# Optimizing a Trainium2 kernel written in Bass

```python
import math
import jax, jax.numpy as jnp
from jax import lax
import numpy as np

D_MODEL = 1024
BATCH = 1
SEQ = 512
DEPTH = 1
DEC_BATCH = 1
DEC_SEQ = 512
PAST_LEN = 128

GRID_W = 64
POOL_WINDOWS = (2, 4, 8, 16)
POOL_GROUP = 128
POOL_WIDTH = POOL_GROUP * len(POOL_WINDOWS)
N_HEADS = 8
N_KV_HEADS = 2
HEAD_DIM = 64
Q_WIDTH = N_HEADS * HEAD_DIM
KV_WIDTH = N_KV_HEADS * HEAD_DIM
ROPE_THETA = 10000.0
Q_BLOCK = 128
IN_WIDTH = POOL_WIDTH + Q_WIDTH + 2 * KV_WIDTH + 2 * D_MODEL
N_KEYS = 128
N_EXPERTS = N_KEYS * N_KEYS
PEER_HEADS = 8
PEER_QDIM = 256
PEER_HALF = PEER_QDIM // 2
PEER_TOPK = 16
TOKEN_CHUNK = 128
EPS = 1e-6

kernel_name = "hybrid_pool_gqa_peer_encoder"

def rmsnorm(x, g):
    xf = x.astype(jnp.float32)
    r = lax.rsqrt(jnp.mean(xf * xf, axis=-1, keepdims=True) + EPS)
    return (xf * r).astype(x.dtype) * g

def pool_mixer(p, pool_w, pool_scale):
    B, T, _ = p.shape
    t = jnp.arange(T)
    outs = []
    for gi, w in enumerate(POOL_WINDOWS):
        xg = p[..., gi * POOL_GROUP:(gi + 1) * POOL_GROUP].astype(jnp.float32)
        cs = jnp.concatenate([jnp.zeros((B, 1, POOL_GROUP), jnp.float32), jnp.cumsum(xg, axis=1)], axis=1)
        lo = jnp.clip(t - w // 2, 0, T)
        hi = jnp.clip(t + w - w // 2, 0, T)
        cnt = (hi - lo).astype(jnp.float32)[None, :, None]
        mean = (jnp.take(cs, hi, axis=1) - jnp.take(cs, lo, axis=1)) / cnt
        outs.append(mean - xg)
    pooled = jnp.stack(outs, axis=2).astype(p.dtype)
    mixed = jnp.einsum('btgc,gcd->btgd', pooled, pool_w).reshape(B, T, POOL_WIDTH)
    return mixed * pool_scale

def axial_rope(x, rows, cols):
    half = HEAD_DIM // 2
    quarter = half // 2
    inv_freq = ROPE_THETA ** (-jnp.arange(quarter, dtype=jnp.float32) / quarter)

    def rot(xs, pos):
        ang = pos.astype(jnp.float32)[:, None] * inv_freq
        cos = jnp.cos(ang)[:, None, :]
        sin = jnp.sin(ang)[:, None, :]
        a = xs[..., :quarter].astype(jnp.float32)
        b = xs[..., quarter:].astype(jnp.float32)
        return jnp.concatenate([a * cos - b * sin, b * cos + a * sin], axis=-1)

    out = jnp.concatenate([rot(x[..., :half], rows), rot(x[..., half:], cols)], axis=-1)
    return out.astype(x.dtype)

def gqa_attention(q, k, v):
    B, T = q.shape[0], q.shape[1]
    nb = T // Q_BLOCK
    grp = N_HEADS // N_KV_HEADS
    qb = q.reshape(B, nb, Q_BLOCK, N_KV_HEADS, grp, HEAD_DIM).transpose(1, 0, 2, 3, 4, 5)
    scale = HEAD_DIM ** -0.5

    def block(qblk):
        s = jnp.einsum('bqkgd,bskd->bkgqs', qblk, k).astype(jnp.float32) * scale
        pr = jax.nn.softmax(s, axis=-1).astype(v.dtype)
        return jnp.einsum('bkgqs,bskd->bqkgd', pr, v)

    o = lax.map(block, qb)
    return o.transpose(1, 0, 2, 3, 4, 5).reshape(B, T, Q_WIDTH)

def peer(h, w_query, sub_keys, expert_u, expert_v):
    B, T, D = h.shape
    n = B * T
    hc = h.reshape(n // TOKEN_CHUNK, TOKEN_CHUNK, D)

    def chunk(xc):
        C = xc.shape[0]
        q = (xc @ w_query).reshape(C, PEER_HEADS, 2, PEER_HALF)
        s = jnp.einsum('chpd,hpkd->chpk', q, sub_keys).astype(jnp.float32)
        sv, si = lax.top_k(s, PEER_TOPK)
        cand = (sv[:, :, 0, :, None] + sv[:, :, 1, None, :]).reshape(C, PEER_HEADS, PEER_TOPK * PEER_TOPK)
        cidx = (si[:, :, 0, :, None] * N_KEYS + si[:, :, 1, None, :]).reshape(C, PEER_HEADS, PEER_TOPK * PEER_TOPK)
        top_s, pos = lax.top_k(cand, PEER_TOPK)
        idx = jnp.take_along_axis(cidx, pos, axis=-1)
        gate = jax.nn.softmax(top_s, axis=-1).astype(xc.dtype)
        u = expert_u[idx]
        a = jnp.einsum('cd,chkd->chk', xc, u)
        hid = jax.nn.gelu(a, approximate=False) * gate
        return jnp.einsum('chk,chkd->cd', hid, expert_v[idx])

    return lax.map(chunk, hc).reshape(B, T, D)

def encoder_layer(x, g_mix, w_in, pool_w, pool_scale, q_norm, k_norm, w_pool_out, w_attn_out, w_out,
                  g_ffn, w_query, sub_keys, expert_u, expert_v):
    B, T, _ = x.shape
    ROWS = T // GRID_W
    rows = jnp.repeat(jnp.arange(ROWS), GRID_W)
    cols = jnp.tile(jnp.arange(GRID_W), ROWS)

    h = rmsnorm(x, g_mix)
    z = h @ w_in
    o1 = POOL_WIDTH
    o2 = o1 + Q_WIDTH
    o3 = o2 + KV_WIDTH
    o4 = o3 + KV_WIDTH
    o5 = o4 + D_MODEL
    p = z[..., :o1]
    q = z[..., o1:o2].reshape(B, T, N_HEADS, HEAD_DIM)
    k = z[..., o2:o3].reshape(B, T, N_KV_HEADS, HEAD_DIM)
    v = z[..., o3:o4].reshape(B, T, N_KV_HEADS, HEAD_DIM)
    gate_pool = jax.nn.sigmoid(z[..., o4:o5])
    gate_attn = jax.nn.sigmoid(z[..., o5:])

    pool_branch = pool_mixer(p, pool_w, pool_scale) @ w_pool_out
    q = axial_rope(rmsnorm(q, q_norm), rows, cols)
    k = axial_rope(rmsnorm(k, k_norm), rows, cols)
    attn_branch = gqa_attention(q, k, v) @ w_attn_out

    merged = gate_pool * pool_branch + gate_attn * attn_branch
    x = x + merged @ w_out
    x = x + peer(rmsnorm(x, g_ffn), w_query, sub_keys, expert_u, expert_v)
    return x

def trunk(x, g_mix, w_in, pool_w, pool_scale, q_norm, k_norm, w_pool_out, w_attn_out, w_out,
          g_ffn, w_query, sub_keys, expert_u, expert_v, g_final):
    for l in range(DEPTH):
        x = encoder_layer(x, g_mix[l], w_in[l], pool_w[l], pool_scale[l], q_norm[l], k_norm[l],
                          w_pool_out[l], w_attn_out[l], w_out[l], g_ffn[l], w_query[l], sub_keys[l],
                          expert_u[l], expert_v[l])
    return rmsnorm(x, g_final)

def setup_inputs(seed: int = 0) -> dict:
    key = jax.random.key(seed)
    ks = jax.random.split(key, 17)
    f32 = jnp.float32
    nrm = lambda k, shape: jax.random.normal(k, shape, f32)
    return {
        "x_prompt": nrm(ks[0], (BATCH, SEQ, D_MODEL)),
        "x_sample": nrm(ks[1], (DEC_BATCH, DEC_SEQ, D_MODEL)),
        "g_mix": 1.0 + 0.05 * nrm(ks[2], (DEPTH, D_MODEL)),
        "w_in": nrm(ks[3], (DEPTH, D_MODEL, IN_WIDTH)) * D_MODEL ** -0.5,
        "pool_w": nrm(ks[4], (DEPTH, len(POOL_WINDOWS), POOL_GROUP, POOL_GROUP)) * POOL_GROUP ** -0.5,
        "pool_scale": 1.0 + 0.1 * nrm(ks[5], (DEPTH, POOL_WIDTH)),
        "q_norm": 1.0 + 0.05 * nrm(ks[6], (DEPTH, HEAD_DIM)),
        "k_norm": 1.0 + 0.05 * nrm(ks[7], (DEPTH, HEAD_DIM)),
        "w_pool_out": nrm(ks[8], (DEPTH, POOL_WIDTH, D_MODEL)) * POOL_WIDTH ** -0.5,
        "w_attn_out": nrm(ks[9], (DEPTH, Q_WIDTH, D_MODEL)) * Q_WIDTH ** -0.5,
        "w_out": nrm(ks[10], (DEPTH, D_MODEL, D_MODEL)) * D_MODEL ** -0.5,
        "g_ffn": 1.0 + 0.05 * nrm(ks[11], (DEPTH, D_MODEL)),
        "w_query": nrm(ks[12], (DEPTH, D_MODEL, PEER_HEADS * PEER_QDIM)) * D_MODEL ** -0.5,
        "sub_keys": nrm(ks[13], (DEPTH, PEER_HEADS, 2, N_KEYS, PEER_HALF)) * PEER_HALF ** -0.5,
        "expert_u": nrm(ks[14], (DEPTH, N_EXPERTS, D_MODEL)) * D_MODEL ** -0.5,
        "expert_v": nrm(ks[15], (DEPTH, N_EXPERTS, D_MODEL)) * 0.25,
        "g_final": 1.0 + 0.05 * nrm(ks[16], (D_MODEL,)),
    }

def reference(x_prompt, x_sample, g_mix, w_in, pool_w, pool_scale, q_norm, k_norm, w_pool_out, w_attn_out,
              w_out, g_ffn, w_query, sub_keys, expert_u, expert_v, g_final):
    y_prompt = trunk(x_prompt, g_mix, w_in, pool_w, pool_scale, q_norm, k_norm, w_pool_out, w_attn_out,
                     w_out, g_ffn, w_query, sub_keys, expert_u, expert_v, g_final)
    y_sample = trunk(x_sample, g_mix, w_in, pool_w, pool_scale, q_norm, k_norm, w_pool_out, w_attn_out,
                     w_out, g_ffn, w_query, sub_keys, expert_u, expert_v, g_final)
    return (y_prompt, y_sample)


_drawn_inputs = setup_inputs


def setup_inputs(seed=0):
    import zlib

    import numpy as np

    out = dict(_drawn_inputs(seed))
    spreads = {}
    factors = {'q_norm': 8.0, 'k_norm': 8.0}
    for name, (base, spread) in spreads.items():
        noise = np.random.default_rng([zlib.crc32(name.encode()), seed]).standard_normal(out[name].shape)
        drawn = base * np.exp(spread * noise) if base else spread * noise
        out[name] = __import__('jax').numpy.asarray(drawn.astype(out[name].dtype))
    for name, factor in factors.items():
        out[name] = (out[name] * factor).astype(out[name].dtype)
    return out
```

```python
from contextlib import ExitStack

import concourse.bass as bass
from concourse import mybir

ALU = mybir.AluOpType
ACT = mybir.ActivationFunctionType
AX = mybir.AxisListType
F32 = mybir.dt.float32
U32 = mybir.dt.uint32

P = 128
BATCHES = 2
T = 512
D = 1024
TT = T // P
KD = D // P
WINDOWS = (2, 4, 8, 16)
GROUPS = len(WINDOWS)
HEADS, KV_HEADS, HD = 8, 2, 64
PAIRS = HEADS // KV_HEADS
POOL_W, Q_W, KV_W = GROUPS * P, HEADS * HD, KV_HEADS * HD
QKV_W = Q_W + 2 * KV_W
QK_HEADS = HEADS + KV_HEADS
GRID_W = 64
ROPE_THETA = 10000.0
PEER_HEADS, N_KEYS, TOPK = 8, 128, 16
HALVES = 2 * PEER_HEADS
EPS = 1e-6
CHUNK = 256
LOWEST = -3.0e38

CAND_RUNS = []
CAND = 0
for _a in range(TOPK):
    _n = TOPK // (_a + 1)
    if CAND_RUNS and CAND_RUNS[-1][2] == _n:
        CAND_RUNS[-1][1] += 1
    else:
        CAND_RUNS.append([_a, 1, _n, CAND])
    CAND += _n

EDGE = 8
BAND_W = 3 * P + 2 * EDGE

BANKS = 6
WSLOTS = 4
RING = 8
BODY = 2 * RING
SUB = 2 * BODY
SLOTS = PEER_HEADS * TOPK
SUBS = SLOTS // SUB
PHASE = TT * SLOTS


def attention_steps():
    return [(t, j, half) for t in range(TT) for j in range(PAIRS) for half in range(KV_HEADS)]


def jobs_of(b):
    for k in range(KD):
        yield (b, "hT", k), None
    for c in range(2):
        for tp in range(2):
            yield (b, "q", c, tp), (b, "q", c)
    for tp in range(2):
        yield (b, "kv", tp), (b, "kv")
    for c in range(2):
        for tp in range(2):
            yield (b, "p", c, tp), (b, "p", c)
    for g in range(GROUPS):
        yield (b, "pooled", g), None
    for g in range(GROUPS):
        yield (b, "mixed", g), None
    for d in range(KD):
        yield (b, "gate_pool", d), (b, "gate_pool", d // 2)
    for d in range(KD):
        yield (b, "pool_out", d), (b, "pool_out", d // 4)
    for j in range(PAIRS):
        yield (b, "qT", j), None
    yield (b, "kT"), None
    n = len(attention_steps())
    yield (b, "s", 0), None
    yield (b, "s", 1), None
    for i in range(n):
        if i + 2 < n:
            yield (b, "s", i + 2), None
        yield (b, "probsT", i), None
    for c in range(KD // 2):
        for d in (2 * c, 2 * c + 1):
            yield (b, "gate_attn", d), (b, "gate_attn", c)
        for d in (2 * c, 2 * c + 1):
            yield (b, "attn_out", d), (b, "attn_out", d // 4)
    for c in range(D // CHUNK):
        for tp in range(2):
            yield (b, "out", c, tp), (b, "out", c)
    for k in range(KD):
        yield (b, "h2T", k), None
    for c in range(HALVES // 2):
        for hp in (2 * c, 2 * c + 1):
            yield (b, "query", hp), (b, "query", c)
        for hp in (2 * c, 2 * c + 1):
            yield (b, "keys", hp), (b, "query", c)


JOB, CHUNKS, LAST_JOB = {}, [], {}
for _b in range(BATCHES):
    for _job, _chunk in jobs_of(_b):
        JOB[_job] = len(JOB)
        if _chunk is not None:
            if _chunk not in LAST_JOB:
                CHUNKS.append(_chunk)
            LAST_JOB[_chunk] = _job


def chunk_order(b):
    return [c for c in CHUNKS if c[0] == b]


def encoder_kernel(nc, x_prompt, x_sample, w_in, pool_w, w_pool_out, w_attn_out, w_out, w_query,
                   keysT, expert_u, expert_v, g_mix, pool_scale, q_norm, k_norm, g_ffn, g_final,
                   ident_c, band_c, rope_c, iota_c, y_prompt, y_sample):
    xs, ys = (x_prompt, x_sample), (y_prompt, y_sample)
    ctx = ExitStack()
    with ctx:
        def sb(name, shape, dt=F32):
            return ctx.enter_context(nc.sbuf_tensor(name, shape, dt))

        def sem(name):
            return ctx.enter_context(nc.semaphore(name))

        def sems(name, n):
            return [sem(f"{name}{i}") for i in range(n)]

        banks = [ctx.enter_context(nc.psum_tensor(f"bank{i}", [P, 512], F32)) for i in range(BANKS)]
        o_banks = [ctx.enter_context(nc.psum_tensor(f"o_bank{i}", [P, PAIRS, P], F32)) for i in range(2)]

        wslot = sb("wslot", [P, WSLOTS, KD * CHUNK])
        keys_sb = sb("keys_sb", [P, WSLOTS, 2 * N_KEYS])
        region_a = sb("region_a", [P, TT * D])
        region_b = sb("region_b", [P, TT * D])
        region_c = sb("region_c", [P, TT * D])
        h2 = sb("h2", [P, TT, D])
        ring = sb("ring", [P, RING, D])
        region_p = sb("region_p", [P, TT * POOL_W])
        region_m = sb("region_m", [P, GROUPS * T])
        region_q = sb("region_q", [P, TT * QKV_W + 2 * QK_HEADS * HD])
        region_s = sb("region_s", [P, 6 * T])
        gate_attn = sb("gate_attn", [P, 2, T])
        ident = sb("ident", [P, P])
        band = sb("band", [P, GROUPS, BAND_W])
        rope = sb("rope", [P, TT, 2, HD])
        iota = sb("iota", [P, CAND])
        pool_w_sb = sb("pool_w_sb", [P, GROUPS, P])
        g_mix_sb = sb("g_mix_sb", [P, KD])
        pool_scale_sb = sb("pool_scale_sb", [P, GROUPS])
        qk_norm_sb = sb("qk_norm_sb", [P, 2, HD])
        g_row = sb("g_row", [P, D])
        idx = sb("idx", [P, BATCHES, TT * SLOTS], U32)
        idx_now = sb("idx_now", [P, 2, RING], U32)
        gate = sb("gate", [P, BATCHES, TT, SLOTS])
        dots = sb("dots", [P, TT * SLOTS])
        dots_now = sb("dots_now", [P, BODY])
        stat = sb("stat", [P, 3, TT])
        head_stat = sb("head_stat", [P, TT, QK_HEADS])
        neg_max = sb("neg_max", [P, 2])
        prob_sum = sb("prob_sum", [P, 2])
        eps = sb("eps", [P, 1])

        xa = region_b[:, :].rearrange("p (t d) -> p t d", t=TT)
        hT = region_a[:, :].rearrange("p (k t) -> p k t", k=KD)
        gate_pool = region_b[:, :].rearrange("p (k t) -> p k t", k=KD)
        merged = gate_pool
        h2T = gate_pool
        x1s = [r[:, :].rearrange("p (t d) -> p t d", t=TT) for r in (region_c, region_a)]
        pool_in = region_p[:, :].rearrange("p (t c) -> p t c", t=TT)
        attnT = region_p[:, :].rearrange("p (j t) -> p j t", j=PAIRS)
        pooledT = region_m[:, :].rearrange("p (g t) -> p g t", g=GROUPS)
        qT = region_m[:, :].rearrange("p (j t) -> p j t", j=PAIRS)
        qkv = region_q[:, 0:TT * QKV_W].rearrange("p (t n) -> p t n", t=TT)
        rope1 = region_q[:, TT * QKV_W:TT * QKV_W + QK_HEADS * HD]
        rope2 = region_q[:, TT * QKV_W + QK_HEADS * HD:]
        junk = region_q[:, 0:D]
        mixedT = region_s[:, 0:GROUPS * T].rearrange("p (g t) -> p g t", g=GROUPS)
        kT = region_s[:, 0:T]
        probs = region_s[:, T:3 * T].rearrange("p (a s) -> p a s", a=2)
        probsT = region_s[:, 3 * T:5 * T].rearrange("p (a s) -> p a s", a=2)
        peer_q = region_s[:, 0:2 * T].rearrange("p (a t) -> p a t", a=2)
        score = region_s[:, 2 * T:6 * T].rearrange("p (a t n) -> p a t n", a=4, t=TT)
        at = [0]

        def scratch(n):
            at[0] += n
            return region_q[:, at[0] - n:at[0]]

        best = scratch(TT * HALVES * TOPK).rearrange("p (t a k) -> p t a k", t=TT, a=HALVES)
        best_at = scratch(TT * HALVES * TOPK // 2).bitcast(mybir.dt.uint16).rearrange(
            "p (t a k) -> p t a k", t=TT, a=HALVES)
        sel_f = scratch(HALVES * TOPK).rearrange("p (a k) -> p a k", a=HALVES)
        cand = scratch(PEER_HEADS * CAND).rearrange("p (h n) -> p h n", h=PEER_HEADS)
        cand_id = scratch(PEER_HEADS * CAND).rearrange("p (h n) -> p h n", h=PEER_HEADS)
        match = scratch(TOPK * CAND)

        bank_filled, bank_freed = sems("bank_filled", BANKS), sems("bank_freed", BANKS)
        o_filled, o_freed = sems("o_filled", 2), sems("o_freed", 2)
        w_loaded = sems("w_loaded", WSLOTS)
        keys_loaded = sems("keys_loaded", WSLOTS)
        x_loaded = sems("x_loaded", TT)
        res_loaded = sem("res_loaded")
        first_loaded, consts_loaded = sem("first_loaded"), sem("consts_loaded")
        g_loaded = sem("g_loaded")
        act_step, dve_step = sem("act_step"), sem("dve_step")
        std_ready = sem("std_ready")
        xr_ready = sem("xr_ready")
        head_sq_ready, head_std_ready, roped = sem("head_sq_ready"), sem("head_std_ready"), sem("roped")
        pool_merged = sem("pool_merged")
        max_ready, exp_ready, probs_ready = sem("max_ready"), sem("exp_ready"), sem("probs_ready")
        merged_ready, x1_ready = sem("merged_ready"), sem("x1_ready")
        std2_ready, h2_ready = sem("std2_ready"), sem("h2_ready")
        halves_done = sem("halves_done")
        top_ready, top_exp = sem("top_ready"), sem("top_exp")
        idx_ready = sem("idx_ready")
        row_landed = sems("row_landed", RING)
        rows_used = sem("rows_used")
        idx_staged, slot_ok = sem("idx_staged"), sem("slot_ok")
        dots_saved, gelu_ready = sem("dots_saved"), sem("gelu_ready")
        std3_ready, y_ready, y_stored = sem("std3_ready"), sem("y_ready"), sem("y_stored")

        def filled(eng, *job):
            n = JOB[job]
            eng.wait_ge(bank_filled[n % BANKS], n // BANKS + 1)
            return banks[n % BANKS]

        def moved(eng, *job):
            n = JOB[job]
            eng.wait_ge(bank_freed[n % BANKS], n // BANKS + 1)

        def frees(*job):
            return bank_freed[JOB[job] % BANKS]

        block = ctx.enter_context(nc.Block())

        @block.sync
        def _(sp):
            def load_x(b):
                if b:
                    filled(sp, b - 1, "query", HALVES - 1)
                for t in range(TT):
                    sp.dma_start(xa[:, t, :], xs[b][0, t * P:(t + 1) * P, :]).then_inc(x_loaded[t], 16)

            def load_residual(b):
                if b:
                    filled(sp, b, "gate_attn", KD - 1)
                sp.dma_start(x1s[b], xs[b][0].rearrange("(t p) d -> p t d", p=P)).then_inc(res_loaded, 16)

            load_x(0)
            sp.dma_start(ident[:], ident_c).then_inc(first_loaded, 16)
            sp.dma_start(g_mix_sb[:], g_mix).then_inc(first_loaded, 16)

            w_in_cols = {"p": 0, "q": POOL_W, "kv": POOL_W + Q_W, "gate_pool": POOL_W + QKV_W,
                         "gate_attn": POOL_W + QKV_W + D}
            for b in range(BATCHES):
                if b:
                    load_x(b)
                for n, chunk in enumerate(chunk_order(b)):
                    m = CHUNKS.index(chunk)
                    if m >= WSLOTS:
                        filled(sp, *LAST_JOB[CHUNKS[m - WSLOTS]])
                    name, c = chunk[1], (chunk[2] if len(chunk) > 2 else 0)
                    dst = wslot[:, m % WSLOTS, :]
                    if name in w_in_cols:
                        at0 = w_in_cols[name] + c * CHUNK
                        src = w_in[:, at0:at0 + CHUNK].rearrange("(k p) n -> p k n", p=P)
                        dst = dst.rearrange("p (k n) -> p k n", k=KD)
                    elif name == "pool_out":
                        src = w_pool_out[:, c * 512:(c + 1) * 512].rearrange("(g p) n -> p g n", p=P)
                        dst = dst.rearrange("p (g n) -> p g n", g=GROUPS)
                    elif name == "attn_out":
                        dst = dst.rearrange("p (j n) -> p j n", j=PAIRS)
                        for half in range(KV_HEADS):
                            src = w_attn_out[half * PAIRS * HD:(half + 1) * PAIRS * HD,
                                             c * 512:(c + 1) * 512].rearrange("(j p) n -> p j n", p=HD)
                            sp.dma_start(dst[half * HD:(half + 1) * HD], src).then_inc(
                                w_loaded[m % WSLOTS], 16)
                        continue
                    else:
                        w = w_out if name == "out" else w_query
                        src = w[:, c * CHUNK:(c + 1) * CHUNK].rearrange("(k p) n -> p k n", p=P)
                        dst = dst.rearrange("p (k n) -> p k n", k=KD)
                    sp.dma_start(dst, src).then_inc(w_loaded[m % WSLOTS], 16)
                    if name == "query":
                        sp.dma_start(keys_sb[:, m % WSLOTS, :],
                                     keysT[:, c * 2 * N_KEYS:(c + 1) * 2 * N_KEYS]).then_inc(
                                         keys_loaded[m % WSLOTS], 16)
                    if b == 0 and n == 3:
                        sp.dma_start(rope[:], rope_c).then_inc(consts_loaded, 16)
                        sp.dma_start(qk_norm_sb[:, 0, :], q_norm.partition_broadcast(P)).then_inc(consts_loaded, 16)
                        sp.dma_start(qk_norm_sb[:, 1, :], k_norm.partition_broadcast(P)).then_inc(consts_loaded, 16)
                        sp.dma_start(band[:], band_c).then_inc(consts_loaded, 16)
                        sp.dma_start(pool_w_sb[:], pool_w.rearrange("g c d -> c g d")).then_inc(consts_loaded, 16)
                        sp.dma_start(pool_scale_sb[:], pool_scale).then_inc(consts_loaded, 16)
                        sp.dma_start(iota[:], iota_c).then_inc(consts_loaded, 16)
                        sp.dma_start(g_row[:], g_ffn.partition_broadcast(P)).then_inc(g_loaded, 16)
                    if name == "out" and c == 1:
                        load_residual(b)
            sp.wait_ge(h2_ready, BATCHES * TT)
            sp.dma_start(g_row[:], g_final.partition_broadcast(P)).then_inc(g_loaded, 16)

        FIRST_ALL, CONSTS_ALL = 2 * 16, 7 * 16

        def chunk_landed(eng, chunk):
            m = CHUNKS.index(chunk)
            count = 0
            for n in range(m % WSLOTS, m + 1, WSLOTS):
                count += 2 if CHUNKS[n][1] == "attn_out" else 1
            eng.wait_ge(w_loaded[m % WSLOTS], 16 * count)
            return m % WSLOTS

        @block.tensor
        def _(pe):
            def fill(*job):
                n = JOB[job]
                if n >= BANKS:
                    pe.wait_ge(bank_freed[n % BANKS], n // BANKS)
                return banks[n % BANKS]

            def done(ins, *job):
                ins.then_inc(bank_filled[JOB[job] % BANKS], 1)

            def turned(job, src):
                bank = fill(*job)
                for t in range(TT):
                    ins = nc.tensor.transpose(bank[:, t * P:(t + 1) * P], src(t), ident[:])
                done(ins, *job)

            def token_major(job, chunk, lhs, tp):
                slot = chunk_landed(pe, chunk)
                w = wslot[:, slot, :].rearrange("p (k n) -> p k n", k=KD)
                bank = fill(*job)
                for tt in range(2):
                    t = 2 * tp + tt
                    for k in range(KD):
                        ins = nc.tensor.matmul(bank[:, tt * CHUNK:(tt + 1) * CHUNK],
                                               lhs[:, k, t * P:(t + 1) * P], w[:, k, :],
                                               start=(k == 0), stop=(k == KD - 1))
                done(ins, *job)

            def feature_major(job, chunk, rhs, col, steps):
                slot = chunk_landed(pe, chunk)
                w = wslot[:, slot, :].rearrange("p (k n) -> p k n", k=steps)
                bank = fill(*job)
                for k in range(steps):
                    ins = nc.tensor.matmul(bank[:], w[:, k, col:col + P], rhs[:, k, :],
                                           start=(k == 0), stop=(k == steps - 1))
                done(ins, *job)

            steps = attention_steps()
            for b in range(BATCHES):
                if b == 0:
                    pe.wait_ge(first_loaded, FIRST_ALL)
                for k in range(KD):
                    if k == 0:
                        pe.wait_ge(xr_ready, TT * (b + 1))
                    turned((b, "hT", k), lambda t: xa[:, t, k * P:(k + 1) * P])
                for k in range(KD):
                    moved(pe, b, "hT", k)
                for c in range(2):
                    for tp in range(2):
                        token_major((b, "q", c, tp), (b, "q", c), hT, tp)
                for tp in range(2):
                    token_major((b, "kv", tp), (b, "kv"), hT, tp)
                for c in range(2):
                    for tp in range(2):
                        token_major((b, "p", c, tp), (b, "p", c), hT, tp)
                if b == 0:
                    pe.wait_ge(consts_loaded, CONSTS_ALL)
                for g in range(GROUPS):
                    for tp in range(2):
                        moved(pe, b, "p", g // 2, tp)
                    bank = fill(b, "pooled", g)
                    for t in range(TT):
                        cols = slice(g * P, (g + 1) * P)
                        kind = 0 if t == 0 else (2 if t == TT - 1 else 1)
                        ins = nc.tensor.matmul(bank[:, t * P:(t + 1) * P], pool_in[:, t, cols],
                                               band[:, g, kind * P:(kind + 1) * P], start=True,
                                               stop=False, skip_group_check=True)
                        if t > 0:
                            ins = nc.tensor.matmul(bank[:, t * P:t * P + EDGE], pool_in[:, t - 1, cols],
                                                   band[:, g, 3 * P:3 * P + EDGE], start=False,
                                                   stop=(t == TT - 1), skip_group_check=True)
                        if t < TT - 1:
                            ins = nc.tensor.matmul(bank[:, (t + 1) * P - EDGE:(t + 1) * P],
                                                   pool_in[:, t + 1, cols],
                                                   band[:, g, 3 * P + EDGE:], start=False,
                                                   stop=True, skip_group_check=True)
                    done(ins, b, "pooled", g)
                for g in range(GROUPS):
                    moved(pe, b, "pooled", g)
                    bank = fill(b, "mixed", g)
                    ins = nc.tensor.matmul(bank[:], pool_w_sb[:, g, :], pooledT[:, g, :], start=True, stop=True)
                    done(ins, b, "mixed", g)
                for d in range(KD):
                    feature_major((b, "gate_pool", d), (b, "gate_pool", d // 2), hT, d % 2 * P, KD)
                for g in range(GROUPS):
                    moved(pe, b, "mixed", g)
                for d in range(KD):
                    feature_major((b, "pool_out", d), (b, "pool_out", d // 4), mixedT, d % 4 * P, GROUPS)
                pe.wait_ge(roped, TT * (b + 1))
                for j in range(PAIRS):
                    turned((b, "qT", j), lambda t: qkv[:, t, j * P:(j + 1) * P])
                turned((b, "kT"), lambda t: qkv[:, t, Q_W:Q_W + KV_W])

                def scores(i):
                    t, j, half = steps[i]
                    if i == 0:
                        moved(pe, b, "kT")
                        for jj in range(PAIRS):
                            moved(pe, b, "qT", jj)
                    bank = fill(b, "s", i)
                    rows = slice(half * HD, (half + 1) * HD)
                    ins = nc.tensor.matmul(bank[:], qT[rows, j, t * P:(t + 1) * P], kT[rows, :],
                                           start=True, stop=True)
                    done(ins, b, "s", i)

                def values(i):
                    t, j, half = steps[i]
                    if j == 0 and half == 0 and b * TT + t >= 2:
                        pe.wait_ge(o_freed[t % 2], (b * TT + t) // 2)
                    moved(pe, b, "probsT", i)
                    for s in range(TT):
                        v = qkv[:, s, Q_W + KV_W + half * HD:Q_W + KV_W + (half + 1) * HD]
                        ins = nc.tensor.matmul(o_banks[t % 2][half * HD:(half + 1) * HD, j, :], v,
                                               probsT[:, i % 2, s * P:(s + 1) * P],
                                               start=(s == 0), stop=(s == TT - 1))
                    if j == PAIRS - 1 and half == 1:
                        ins.then_inc(o_filled[t % 2], 1)

                scores(0)
                scores(1)
                for i in range(len(steps)):
                    if i + 2 < len(steps):
                        scores(i + 2)
                    pe.wait_ge(probs_ready, b * len(steps) + i + 1)
                    turned((b, "probsT", i), lambda s: probs[:, i % 2, s * P:(s + 1) * P])
                    if i:
                        values(i - 1)
                values(len(steps) - 1)
                for c in range(KD // 2):
                    for d in (2 * c, 2 * c + 1):
                        feature_major((b, "gate_attn", d), (b, "gate_attn", c), hT, d % 2 * P, KD)
                    if c == 0:
                        for t in range(2):
                            pe.wait_ge(o_freed[t], (b + 1) * TT // 2)
                    for d in (2 * c, 2 * c + 1):
                        feature_major((b, "attn_out", d), (b, "attn_out", d // 4), attnT, d % 4 * P, PAIRS)
                pe.wait_ge(merged_ready, KD * (b + 1))
                for c in range(D // CHUNK):
                    for tp in range(2):
                        token_major((b, "out", c, tp), (b, "out", c), merged, tp)
                pe.wait_ge(h2_ready, TT * (b + 1))
                for k in range(KD):
                    turned((b, "h2T", k), lambda t: h2[:, t, k * P:(k + 1) * P])
                for k in range(KD):
                    moved(pe, b, "h2T", k)
                for c in range(HALVES // 2):
                    for hp in (2 * c, 2 * c + 1):
                        feature_major((b, "query", hp), (b, "query", c), h2T, hp % 2 * P, KD)
                    m = CHUNKS.index((b, "query", c))
                    pe.wait_ge(keys_loaded[m % WSLOTS],
                               16 * sum(CHUNKS[n][1] == "query" for n in range(m % WSLOTS, m + 1, WSLOTS)))
                    for hp in (2 * c, 2 * c + 1):
                        moved(pe, b, "query", hp)
                        bank = fill(b, "keys", hp)
                        for t in range(TT):
                            ins = nc.tensor.matmul(bank[:, t * P:(t + 1) * P],
                                                   peer_q[:, hp % 2, t * P:(t + 1) * P],
                                                   keys_sb[:, m % WSLOTS, hp % 2 * N_KEYS:(hp % 2 + 1) * N_KEYS],
                                                   start=True, stop=True)
                        done(ins, b, "keys", hp)

        @block.scalar
        def _(act):
            n_act = [0]

            def link(ins):
                n_act[0] += 1
                ins.then_inc(act_step, 1)
                act.wait_ge(act_step, n_act[0])

            def move(dst, job, func=ACT.Identity, scale=1.0, view=None):
                bank = filled(act, *job)
                src = bank[:] if view is None else view(bank)
                nc.scalar.activation(dst, src, func, scale=scale).then_inc(frees(*job), 1)

            def norm1(b):
                if b:
                    act.wait_ge(idx_ready, TT * b)
                for t in range(TT):
                    act.wait_ge(x_loaded[t], 16 * (b + 1))
                    link(nc.scalar.activation(junk, xa[:, t, :], ACT.Square, accum_out=stat[:, 0, t:t + 1]))
                nc.scalar.activation(stat[:, 0, :], stat[:, 0, :], ACT.Sqrt, bias=eps[:],
                                     scale=1.0 / D).then_inc(std_ready, 1)

            def projections(b):
                if b == 0:
                    act.wait_ge(first_loaded, FIRST_ALL)
                for k in range(KD):
                    move(hT[:, k, :], (b, "hT", k), scale=g_mix_sb[:, k:k + 1])
                pair = lambda bank: bank[:].rearrange("p (t n) -> p t n", t=2)
                for c in range(2):
                    for tp in range(2):
                        move(qkv[:, 2 * tp:2 * tp + 2, c * CHUNK:(c + 1) * CHUNK], (b, "q", c, tp), view=pair)
                for tp in range(2):
                    move(qkv[:, 2 * tp:2 * tp + 2, Q_W:QKV_W], (b, "kv", tp), view=pair)
                for c in range(2):
                    for tp in range(2):
                        move(pool_in[:, 2 * tp:2 * tp + 2, c * CHUNK:(c + 1) * CHUNK], (b, "p", c, tp), view=pair)
                act.wait_ge(head_sq_ready, b + 1)
                nc.scalar.activation(head_stat[:], head_stat[:], ACT.Sqrt, bias=eps[:],
                                     scale=1.0 / HD).then_inc(head_std_ready, 1)
                for g in range(GROUPS):
                    move(pooledT[:, g, :], (b, "pooled", g))
                if b == 0:
                    act.wait_ge(consts_loaded, CONSTS_ALL)
                for g in range(GROUPS):
                    move(mixedT[:, g, :], (b, "mixed", g), scale=pool_scale_sb[:, g:g + 1])
                for d in range(KD):
                    move(gate_pool[:, d, :], (b, "gate_pool", d), ACT.Sigmoid)

            def attention(b):
                n = len(attention_steps())
                for j in range(PAIRS):
                    move(qT[:, j, :], (b, "qT", j), scale=HD ** -0.5)
                move(kT, (b, "kT"))

                def exp(i):
                    bank = filled(act, b, "s", i)
                    act.wait_ge(max_ready, b * n + i + 1)
                    if i >= 2:
                        filled(act, b, "probsT", i - 2)
                    nc.scalar.activation(probs[:, i % 2, :], bank[:], ACT.Exp, bias=neg_max[:, i % 2:i % 2 + 1],
                                         accum_out=prob_sum[:, i % 2:i % 2 + 1]).then_inc(exp_ready, 1)

                exp(0)
                for i in range(n):
                    if i + 1 < n:
                        exp(i + 1)
                    move(probsT[:, i % 2, :], (b, "probsT", i))
                    if i % HEADS == 0 and i:
                        outputs(b, i // HEADS - 1)
                outputs(b, TT - 1)

            def outputs(b, t):
                act.wait_ge(o_filled[t % 2], (b * TT + t) // 2 + 1)
                nc.scalar.activation(attnT[:, :, t * P:(t + 1) * P], o_banks[t % 2][:],
                                     ACT.Identity).then_inc(o_freed[t % 2], 1)

            def gates(b):
                for d in range(KD):
                    if d >= 2:
                        act.wait_ge(merged_ready, b * KD + d - 1)
                    move(gate_attn[:, d % 2, :], (b, "gate_attn", d), ACT.Sigmoid)

            def norm2(b):
                for t in range(TT):
                    act.wait_ge(x1_ready, b * 8 + 8)
                    link(nc.scalar.activation(junk, x1s[b][:, t, :], ACT.Square, accum_out=stat[:, 1, t:t + 1]))
                nc.scalar.activation(stat[:, 1, :], stat[:, 1, :], ACT.Sqrt, bias=eps[:],
                                     scale=1.0 / D).then_inc(std2_ready, 1)

            def queries(b):
                for k in range(KD):
                    move(h2T[:, k, :], (b, "h2T", k))
                for c in range(HALVES // 2):
                    for hp in (2 * c, 2 * c + 1):
                        move(peer_q[:, hp % 2, :], (b, "query", hp))
                    for hp in (2 * c, 2 * c + 1):
                        if hp >= 4:
                            act.wait_ge(halves_done, b * HALVES + hp - 3)
                        move(score[:, hp % 4, :, :], (b, "keys", hp),
                             view=lambda bank: bank[:].rearrange("p (t n) -> p t n", t=TT))

            def gate_exp(b, t):
                act.wait_ge(top_ready, b * TT + t + 1)
                g = gate[:, b, t, :]
                nc.scalar.activation(g, g, ACT.Exp).then_inc(top_exp, 1)

            def gelu(b):
                act.wait_ge(dots_saved, (b + 1) * PHASE // BODY)
                nc.scalar.activation(dots[:], dots[:], ACT.Gelu).then_inc(gelu_ready, 1)

            def finish(b, t):
                act.wait_ge(rows_used, RING + (2 * b + 1) * PHASE + (t + 1) * SLOTS)
                link(nc.scalar.activation(junk, x1s[b][:, t, :], ACT.Square, accum_out=stat[:, 2, t:t + 1]))
                nc.scalar.activation(stat[:, 2, t:t + 1], stat[:, 2, t:t + 1], ACT.Sqrt, bias=eps[:],
                                     scale=1.0 / D).then_inc(std3_ready, 1)
                act.wait_ge(y_ready, b * TT + t + 1)
                act.dma_start(ys[b][0, t * P:(t + 1) * P, :], x1s[b][:, t, :]).then_inc(y_stored, 16)

            act.wait_ge(dve_step, 1)
            norm1(0)
            projections(0)
            attention(0)
            gates(0)
            norm2(0)
            queries(0)
            for t in range(TT):
                gate_exp(0, t)
            norm1(1)
            projections(1)
            attention(1)
            gelu(0)
            gates(1)
            norm2(1)
            queries(1)
            for t in range(TT):
                gate_exp(1, t)
            for t in range(TT):
                finish(0, t)
            gelu(1)
            for t in range(TT):
                finish(1, t)
            act.wait_ge(y_stored, 16 * BATCHES * TT)

        @block.gpsimd
        def _(pool):
            for b in range(BATCHES):
                for phase, table in enumerate((expert_u, expert_v)):
                    base = (2 * b + phase) * PHASE
                    for t in range(TT):
                        pool.wait_ge(idx_ready, b * TT + t + 1)
                        with pool.Fori(0, SLOTS // BODY) as i:
                            for half in range(2):
                                n0 = i * BODY + base + t * SLOTS + half * RING
                                pool.wait_ge(rows_used, n0 + 1)
                                pool.sem_inc(slot_ok, 1)
                                nc.gpsimd.tensor_copy(
                                    idx_now[:, half, :],
                                    idx[:, b, bass.ds(i * BODY + t * SLOTS + half * RING, RING)]).then_inc(idx_staged, 1)
                                pool.wait_ge(idx_staged, (i * 2 + half + 1) + (base + t * SLOTS) // RING)
                                for r in range(RING):
                                    pool.wait_ge(rows_used, n0 + r + 1)
                                    pool.sem_inc(slot_ok, 1)
                                    nc.gpsimd.indirect_dma_start(
                                        ring[:, r, :], None, table,
                                        bass.IndirectOffsetOnAxis(ap=idx_now[:, half, r:r + 1], axis=0)).then_inc(row_landed[r], 16)

        @block.vector
        def _(dve):
            n_dve = [0]

            def step(ins):
                n_dve[0] += 1
                ins.then_inc(dve_step, 1)

            def sync():
                dve.wait_ge(dve_step, n_dve[0])

            def link(ins):
                step(ins)
                sync()

            def norm1(b):
                dve.wait_ge(std_ready, b + 1)
                link(nc.vector.reciprocal(stat[:, 0, :], stat[:, 0, :]))
                for t in range(TT):
                    nc.vector.tensor_scalar(xa[:, t, :], xa[:, t, :], stat[:, 0, t:t + 1], None,
                                            ALU.mult).then_inc(xr_ready, 1)

            def rotate(b):
                if b == 0:
                    dve.wait_ge(consts_loaded, CONSTS_ALL)
                for t in range(TT):
                    if t % 2 == 0:
                        for c in range(2):
                            moved(dve, b, "q", c, t // 2)
                        moved(dve, b, "kv", t // 2)
                    qk = qkv[:, t, 0:Q_W + KV_W]
                    link(nc.vector.tensor_tensor(rope1, qk, qk, ALU.mult))
                    link(nc.vector.tensor_reduce(head_stat[:, t, :], rope1.rearrange("p (h d) -> p h d", d=HD),
                                                 AX.X, ALU.add))
                dve.sem_inc(head_sq_ready, 1)
                dve.wait_ge(head_std_ready, b + 1)
                link(nc.vector.reciprocal(head_stat[:], head_stat[:]))
                for t in range(TT):
                    heads = qkv[:, t, 0:Q_W + KV_W].rearrange("p (h d) -> p h d", d=HD)
                    r1, r2 = (r.rearrange("p (h d) -> p h d", d=HD) for r in (rope1, rope2))
                    link(nc.vector.tensor_tensor(r1, heads, head_stat[:, t, :].unsqueeze(2).to_broadcast(
                        [P, QK_HEADS, HD]), ALU.mult))
                    step(nc.vector.tensor_tensor(heads[:, 0:HEADS, :], r1[:, 0:HEADS, :],
                                                 qk_norm_sb[:, 0:1, :].to_broadcast([P, HEADS, HD]), ALU.mult))
                    link(nc.vector.tensor_tensor(heads[:, HEADS:, :], r1[:, HEADS:, :],
                                                 qk_norm_sb[:, 1:2, :].to_broadcast([P, KV_HEADS, HD]), ALU.mult))
                    step(nc.vector.tensor_tensor(r1, heads, rope[:, t, 0:1, :].to_broadcast([P, QK_HEADS, HD]),
                                                 ALU.mult))
                    for q in range(2):
                        src = heads.rearrange("p h (a q d) -> p h a q d", a=2, q=2)[:, :, :, 1 - q, :]
                        dst = r2.rearrange("p h (a q d) -> p h a q d", a=2, q=2)[:, :, :, q, :]
                        sin = rope[:, t, 1:2, :].rearrange("p o (a q d) -> p o a q d", a=2, q=2)[:, :, :, q, :]
                        step(nc.vector.tensor_tensor(dst, src, sin.to_broadcast([P, QK_HEADS, 2, HD // 4]), ALU.mult))
                    sync()
                    pairs = qkv[:, t, 0:Q_W].rearrange("p (j a d) -> p a j d", j=PAIRS, d=HD)
                    for half in range(KV_HEADS):
                        hs = slice(half * PAIRS, (half + 1) * PAIRS)
                        step(nc.vector.tensor_tensor(pairs[:, half], r1[:, hs, :], r2[:, hs, :], ALU.add))
                    link(nc.vector.tensor_tensor(heads[:, HEADS:, :], r1[:, HEADS:, :], r2[:, HEADS:, :], ALU.add))
                    dve.sem_inc(roped, 1)

            def pool_out(b):
                for d in range(KD):
                    bank = filled(dve, b, "pool_out", d)
                    nc.vector.tensor_tensor(merged[:, d, :], gate_pool[:, d, :], bank[:],
                                            ALU.mult).then_inc(frees(b, "pool_out", d), 1)

            n_att = len(attention_steps())

            def row_max(b, i):
                bank = filled(dve, b, "s", i)
                if i >= 2:
                    dve.wait_ge(exp_ready, b * n_att + i - 1)
                nc.vector.tensor_reduce(neg_max[:, i % 2:i % 2 + 1], bank[:], AX.X, ALU.max,
                                        negate=True).then_inc(max_ready, 1)

            def normalise(b, i):
                dve.wait_ge(exp_ready, b * n_att + i + 1)
                link_free = nc.vector.reciprocal(prob_sum[:, i % 2:i % 2 + 1], prob_sum[:, i % 2:i % 2 + 1])
                link_free.then_inc(frees(b, "s", i), 1)
                moved(dve, b, "s", i)
                nc.vector.tensor_scalar(probs[:, i % 2, :], probs[:, i % 2, :], prob_sum[:, i % 2:i % 2 + 1],
                                        None, ALU.mult).then_inc(probs_ready, 1)

            def attention(b, first, last):
                if first == 0:
                    row_max(b, 0)
                for i in range(first, last):
                    if i + 1 < n_att:
                        row_max(b, i + 1)
                    normalise(b, i)

            def attn_out(b, first, last):
                for d in range(first, last):
                    moved(dve, b, "gate_attn", d)
                    bank = filled(dve, b, "attn_out", d)
                    g = gate_attn[:, d % 2, :]
                    nc.vector.tensor_tensor(g, g, bank[:], ALU.mult).then_inc(frees(b, "attn_out", d), 1)
                    moved(dve, b, "attn_out", d)
                    nc.vector.tensor_tensor(merged[:, d, :], merged[:, d, :], g, ALU.add).then_inc(merged_ready, 1)

            def out(b):
                dve.wait_ge(res_loaded, 16 * (b + 1))
                for c in range(D // CHUNK):
                    for tp in range(2):
                        bank = filled(dve, b, "out", c, tp)
                        x = x1s[b][:, 2 * tp:2 * tp + 2, c * CHUNK:(c + 1) * CHUNK]
                        ins = nc.vector.tensor_tensor(x, x, bank[:].rearrange("p (t n) -> p t n", t=2), ALU.add)
                        ins.then_inc(frees(b, "out", c, tp), 1)
                for c in range(D // CHUNK):
                    for tp in range(2):
                        moved(dve, b, "out", c, tp)
                dve.sem_inc(x1_ready, 8)

            def norm2(b):
                if b == 0:
                    dve.wait_ge(g_loaded, 16)
                dve.wait_ge(std2_ready, b + 1)
                link(nc.vector.reciprocal(stat[:, 1, :], stat[:, 1, :]))
                for t in range(TT):
                    nc.vector.scalar_tensor_tensor(out=h2[:, t, :], in0=x1s[b][:, t, :], scalar=stat[:, 1, t:t + 1],
                                                   in1=g_row[:], op0=ALU.mult, op1=ALU.mult).then_inc(h2_ready, 1)

            def top_halves(b, hp):
                moved(dve, b, "keys", hp)
                s = score[:, hp % 4]
                for t in range(TT):
                    step(nc.vector.max(best[:, t, hp, 0:8], s[:, t, :]))
                sync()
                for t in range(TT):
                    step(nc.vector.max_index(best_at[:, t, hp, 0:8], best[:, t, hp, 0:8], s[:, t, :]))
                sync()
                for t in range(TT):
                    step(nc.vector.match_replace(s[:, t, :], best[:, t, hp, 0:8], s[:, t, :], LOWEST))
                sync()
                for t in range(TT):
                    step(nc.vector.max(best[:, t, hp, 8:16], s[:, t, :]))
                sync()
                for t in range(TT):
                    ins = nc.vector.max_index(best_at[:, t, hp, 8:16], best[:, t, hp, 8:16], s[:, t, :])
                ins.then_inc(halves_done, 1)

            def candidates(out, first, second):
                for a, rows, cols, off in CAND_RUNS:
                    dst = out[:, :, off:off + rows * cols]
                    left, right = first[:, :, a:a + rows], second[:, :, 0:cols]
                    if cols == 1:
                        right = right.to_broadcast([P, PEER_HEADS, rows])
                    elif rows == 1:
                        left = left.to_broadcast([P, PEER_HEADS, cols])
                    else:
                        dst = dst.rearrange("p h (a b) -> p h a b", b=cols)
                        left = left.unsqueeze(3).to_broadcast([P, PEER_HEADS, rows, cols])
                        right = right.unsqueeze(2).to_broadcast([P, PEER_HEADS, rows, cols])
                    step(nc.vector.tensor_tensor(dst, left, right, ALU.add))

            def merge(b, t):
                if t == 0:
                    dve.wait_ge(halves_done, HALVES * (b + 1))
                ids = sel_f
                view = best_at[:, t].rearrange("p (h a) k -> p h a k", a=2)
                idv = ids.rearrange("p (h a) k -> p h a k", a=2)
                val = best[:, t].rearrange("p (h a) k -> p h a k", a=2)
                step(nc.vector.tensor_scalar(idv[:, :, 0, :], view[:, :, 0, :], float(N_KEYS), None, ALU.mult))
                step(nc.vector.tensor_copy(idv[:, :, 1, :], view[:, :, 1, :]))
                candidates(cand, val[:, :, 0, :], val[:, :, 1, :])
                sync()
                candidates(cand_id, idv[:, :, 0, :], idv[:, :, 1, :])
                top = gate[:, b, t, :].rearrange("p (h k) -> p h k", k=TOPK)
                pos_i = best_at[:, t].rearrange("p (a h) k -> p a h k", a=2)[:, 0]
                for h in range(PEER_HEADS):
                    step(nc.vector.max(top[:, h, 0:8], cand[:, h, :]))
                sync()
                for h in range(PEER_HEADS):
                    step(nc.vector.max_index(pos_i[:, h, 0:8], top[:, h, 0:8], cand[:, h, :]))
                sync()
                for h in range(PEER_HEADS):
                    step(nc.vector.match_replace(cand[:, h, :], top[:, h, 0:8], cand[:, h, :], LOWEST))
                sync()
                for h in range(PEER_HEADS):
                    step(nc.vector.max(top[:, h, 8:16], cand[:, h, :]))
                sync()
                for h in range(PEER_HEADS):
                    step(nc.vector.max_index(pos_i[:, h, 8:16], top[:, h, 8:16], cand[:, h, :]))
                sync()
                pos = sel_f[:, 0:PEER_HEADS, :]
                found = sel_f[:, PEER_HEADS:, :]
                link(nc.vector.tensor_copy(pos, pos_i))
                for h in range(PEER_HEADS):
                    hit = match.rearrange("p (k n) -> p k n", n=CAND)
                    link(nc.vector.tensor_tensor(hit, pos[:, h, :].unsqueeze(2).to_broadcast([P, TOPK, CAND]),
                                                 iota[:].unsqueeze(1).to_broadcast([P, TOPK, CAND]), ALU.is_equal))
                    link(nc.vector.tensor_tensor(hit, hit, cand_id[:, h:h + 1, :].to_broadcast([P, TOPK, CAND]),
                                                 ALU.mult))
                    link(nc.vector.tensor_reduce(found[:, h, :], hit, AX.X, ALU.add))
                nc.vector.tensor_copy(idx[:, b, t * SLOTS:(t + 1) * SLOTS].rearrange("p (h k) -> p h k", k=TOPK),
                                      found).then_inc(idx_ready, 1)
                link(nc.vector.tensor_copy(cand[:, :, 0:1], top[:, :, 0:1]))
                nc.vector.tensor_tensor(top, top, cand[:, :, 0:1].to_broadcast([P, PEER_HEADS, TOPK]),
                                        ALU.subtract).then_inc(top_ready, 1)
                dve.wait_ge(top_exp, b * TT + t + 1)
                link(nc.vector.tensor_reduce(cand[:, :, 0], top, AX.X, ALU.add))
                link(nc.vector.reciprocal(cand[:, :, 0], cand[:, :, 0]))
                link(nc.vector.tensor_tensor(top, top, cand[:, :, 0:1].to_broadcast([P, PEER_HEADS, TOPK]), ALU.mult))

            def dot_rows(b, t, sub):
                base = 2 * b * PHASE + t * SLOTS + sub * SUB
                with dve.Fori(0, SUB // BODY) as i:
                    for s in range(BODY):
                        r = s % RING
                        dve.wait_ge(row_landed[r], (i * 2 + (base // RING + s // RING + 1)) * 16)
                        nc.vector.tensor_tensor_reduce(ring[:, r, :], ring[:, r, :], h2[:, t, :], 1.0, 0.0, ALU.mult,
                                                       ALU.add, dots_now[:, s:s + 1]).then_inc(rows_used, 1)
                    dve.wait_ge(rows_used, i * BODY + (RING + base + BODY))
                    nc.vector.tensor_copy(dots[:, bass.ds(i * BODY + (t * SLOTS + sub * SUB), BODY)],
                                          dots_now[:]).then_inc(dots_saved, 1)
                    dve.wait_ge(dots_saved, i + ((b * PHASE + t * SLOTS + sub * SUB) // BODY + 1))

            def weigh(b):
                dve.wait_ge(gelu_ready, b + 1)
                link(nc.vector.tensor_tensor(dots[:], dots[:], gate[:, b].rearrange("p t n -> p (t n)"), ALU.mult))

            def add_rows(b, t, sub):
                base = (2 * b + 1) * PHASE + t * SLOTS + sub * SUB
                with dve.Fori(0, SUB // BODY) as i:
                    for s in range(BODY):
                        r = s % RING
                        dve.wait_ge(row_landed[r], (i * 2 + (base // RING + s // RING + 1)) * 16)
                        dve.wait_ge(rows_used, i * BODY + (RING + base + s))
                        nc.vector.scalar_tensor_tensor(
                            out=x1s[b][:, t, :], in0=ring[:, r, :],
                            scalar=dots[:, bass.ds(i * BODY + (t * SLOTS + sub * SUB + s), 1)],
                            in1=x1s[b][:, t, :], op0=ALU.mult, op1=ALU.add).then_inc(rows_used, 1)

            def finish(b, t):
                dve.wait_ge(g_loaded, 32)
                dve.wait_ge(std3_ready, b * TT + t + 1)
                link(nc.vector.reciprocal(stat[:, 2, t:t + 1], stat[:, 2, t:t + 1]))
                nc.vector.scalar_tensor_tensor(out=x1s[b][:, t, :], in0=x1s[b][:, t, :], scalar=stat[:, 2, t:t + 1],
                                               in1=g_row[:], op0=ALU.mult, op1=ALU.mult).then_inc(y_ready, 1)

            step(nc.vector.memset(eps[:], EPS))
            dve.sem_inc(rows_used, RING)
            norm1(0)
            rotate(0)
            pool_out(0)
            attention(0, 0, n_att)
            attn_out(0, 0, KD)
            out(0)
            norm2(0)
            for hp in range(HALVES):
                top_halves(0, hp)
            merge(0, 0)

            between_dots = ([lambda t=t: merge(0, t) for t in range(1, TT)]
                            + [lambda: norm1(1), None, lambda: rotate(1), lambda: pool_out(1)]
                            + [lambda i=i: attention(1, 4 * i, 4 * i + 4) for i in range(8)])
            between_sums = ([None, lambda: (attn_out(1, 0, KD), out(1)), lambda: norm2(1)]
                            + [lambda i=i: (top_halves(1, 2 * i), top_halves(1, 2 * i + 1)) for i in range(8)]
                            + [lambda t=t: merge(1, t) for t in range(TT)])
            for n in range(TT * SUBS):
                dot_rows(0, n // SUBS, n % SUBS)
                if n < len(between_dots) and between_dots[n]:
                    between_dots[n]()
            weigh(0)
            for n in range(TT * SUBS):
                add_rows(0, n // SUBS, n % SUBS)
                if n < len(between_sums) and between_sums[n]:
                    between_sums[n]()
            for t in range(TT):
                finish(0, t)

            for n in range(TT * SUBS):
                dot_rows(1, n // SUBS, n % SUBS)
            weigh(1)
            for t in range(TT):
                for sub in range(SUBS):
                    add_rows(1, t, sub)
                finish(1, t)


def shape_constants(np):
    band = np.zeros((P, GROUPS, BAND_W), np.float32)
    s, t = np.arange(T)[:, None], np.arange(T)[None, :]
    for g, w in enumerate(WINDOWS):
        lo, hi = np.clip(t - w // 2, 0, T), np.clip(t + w - w // 2, 0, T)
        m = ((s >= lo) & (s < hi)) / (hi - lo).astype(np.float32) - (s == t)
        for kind, tile in enumerate((0, 1, TT - 1)):
            band[:, g, kind * P:(kind + 1) * P] = m[tile * P:(tile + 1) * P, tile * P:(tile + 1) * P]
        band[:, g, 3 * P:3 * P + EDGE] = m[0:P, P:P + EDGE]
        band[:, g, 3 * P + EDGE:] = m[P:2 * P, P - EDGE:P]
    quarter = HD // 4
    inv = np.float32(ROPE_THETA) ** (-np.arange(quarter, dtype=np.float32) / np.float32(quarter))
    rope = np.zeros((P, TT, 2, 2, 2, quarter), np.float32)
    tok = np.arange(T).reshape(TT, P).T
    for axis, pos in enumerate((tok // GRID_W, tok % GRID_W)):
        ang = pos.astype(np.float32)[:, :, None] * inv.astype(np.float32)
        rope[:, :, 0, axis] = np.cos(ang)[:, :, None]
        rope[:, :, 1, axis, 0] = -np.sin(ang)
        rope[:, :, 1, axis, 1] = np.sin(ang)
    iota = np.broadcast_to(np.arange(CAND, dtype=np.float32), (P, CAND))
    return {"ident_c": np.eye(P, dtype=np.float32), "band_c": band,
            "rope_c": rope.reshape(P, TT, 2, HD), "iota_c": np.ascontiguousarray(iota)}


def kernel(**inputs):
    import numpy as np
    import concourse.bacc as bacc
    from concourse.bass_utils import run_bass_kernel_spmd

    a = {k: np.asarray(v) for k, v in inputs.items()}
    columns = lambda v, n: np.ascontiguousarray(v.reshape(n, P).T)
    arrays = {
        "x_prompt": a["x_prompt"], "x_sample": a["x_sample"], "w_in": a["w_in"][0], "pool_w": a["pool_w"][0],
        "w_pool_out": a["w_pool_out"][0], "w_attn_out": a["w_attn_out"][0], "w_out": a["w_out"][0],
        "w_query": a["w_query"][0],
        "keysT": a["sub_keys"][0].reshape(HALVES * N_KEYS, P).T,
        "expert_u": a["expert_u"][0], "expert_v": a["expert_v"][0],
        "g_mix": columns(a["g_mix"][0], KD), "pool_scale": columns(a["pool_scale"][0], GROUPS),
        "q_norm": a["q_norm"][0], "k_norm": a["k_norm"][0], "g_ffn": a["g_ffn"][0], "g_final": a["g_final"],
        **shape_constants(np),
    }
    nc = bacc.Bacc("TRN2", target_bir_lowering=False, num_devices=1)
    given, args = {}, []
    for name, v in arrays.items():
        v = np.ascontiguousarray(v)
        given[f"in_{name}"] = v
        args.append(nc.dram_tensor(f"in_{name}", v.shape, mybir.dt.from_np(v.dtype), kind="ExternalInput").ap())
    for n in range(BATCHES):
        args.append(nc.dram_tensor(f"out_{n}", (1, T, D), F32, kind="ExternalOutput").ap())
    encoder_kernel(nc, *args)
    r = run_bass_kernel_spmd(nc, [given], core_ids=[0])
    return tuple(r.results[0][f"out_{n}"] for n in range(BATCHES))
```

```python
from contextlib import ExitStack

import concourse.bass as bass
from concourse import mybir

ALU = mybir.AluOpType
ACT = mybir.ActivationFunctionType
AX = mybir.AxisListType
F32 = mybir.dt.float32
U32 = mybir.dt.uint32

P = 128
BATCHES = 2
T = 512
D = 1024
TT = T // P
KD = D // P
WINDOWS = (2, 4, 8, 16)
GROUPS = len(WINDOWS)
HEADS, KV_HEADS, HD = 8, 2, 64
PAIRS = HEADS // KV_HEADS
POOL_W, Q_W, KV_W = GROUPS * P, HEADS * HD, KV_HEADS * HD
QKV_W = Q_W + 2 * KV_W
QK_HEADS = HEADS + KV_HEADS
GRID_W = 64
ROPE_THETA = 10000.0
PEER_HEADS, N_KEYS, TOPK = 8, 128, 16
HALVES = 2 * PEER_HEADS
EPS = 1e-6
CHUNK = 256
LOWEST = -3.0e38

CAND_RUNS = []
CAND = 0
for _a in range(TOPK):
    _n = TOPK // (_a + 1)
    if CAND_RUNS and CAND_RUNS[-1][2] == _n:
        CAND_RUNS[-1][1] += 1
    else:
        CAND_RUNS.append([_a, 1, _n, CAND])
    CAND += _n

EDGE = 8
BAND_W = 3 * P + 2 * EDGE

BANKS = 6
WSLOTS = 4
RING = 8
BODY = 2 * RING
SUB = 2 * BODY
SLOTS = PEER_HEADS * TOPK
SUBS = SLOTS // SUB
GATHERED = (TT, 1)
DENSE = TT - GATHERED[1]
DENSE_T = DENSE * P
PHASE_START = {(0, 0): 0, (0, 1): GATHERED[0] * SLOTS, (1, 0): 2 * GATHERED[0] * SLOTS,
               (1, 1): (2 * GATHERED[0] + GATHERED[1]) * SLOTS}
BLOCK = 32
BLOCKS = DENSE_T // BLOCK
OH_RING = 8
COLS_BESIDE = {(0, 1): 6, (1, 0): 4, (1, 1): 4}
COLS_START = {(0, 1): 0}
COLS_START[(1, 0)] = COLS_START[(0, 1)] + GATHERED[0] * SUBS * COLS_BESIDE[(0, 1)]
COLS_START[(1, 1)] = COLS_START[(1, 0)] + GATHERED[1] * SUBS * COLS_BESIDE[(1, 0)]
assert COLS_START[(1, 1)] + GATHERED[1] * SUBS * COLS_BESIDE[(1, 1)] == N_KEYS


def attention_steps():
    return [(t, j, half) for t in range(TT) for j in range(PAIRS) for half in range(KV_HEADS)]


def jobs_of(b):
    for k in range(KD):
        yield (b, "hT", k), None
    for c in range(2):
        for tp in range(2):
            yield (b, "q", c, tp), (b, "q", c)
    for tp in range(2):
        yield (b, "kv", tp), (b, "kv")
    for c in range(2):
        for tp in range(2):
            yield (b, "p", c, tp), (b, "p", c)
    for g in range(GROUPS):
        yield (b, "pooled", g), None
    for g in range(GROUPS):
        yield (b, "mixed", g), None
    for d in range(KD):
        yield (b, "gate_pool", d), (b, "gate_pool", d // 2)
    for d in range(KD):
        yield (b, "pool_out", d), (b, "pool_out", d // 4)
    for j in range(PAIRS):
        yield (b, "qT", j), None
    yield (b, "kT"), None
    n = len(attention_steps())
    yield (b, "s", 0), None
    yield (b, "s", 1), None
    for i in range(n):
        if i + 2 < n:
            yield (b, "s", i + 2), None
        yield (b, "probsT", i), None
    for c in range(KD // 2):
        for d in (2 * c, 2 * c + 1):
            yield (b, "gate_attn", d), (b, "gate_attn", c)
        for d in (2 * c, 2 * c + 1):
            yield (b, "attn_out", d), (b, "attn_out", d // 4)
    for c in range(D // CHUNK):
        for tp in range(2):
            yield (b, "out", c, tp), (b, "out", c)
    for k in range(KD):
        yield (b, "h2T", k), None
    for c in range(HALVES // 2):
        for hp in (2 * c, 2 * c + 1):
            yield (b, "query", hp), (b, "query", c)
        for hp in (2 * c, 2 * c + 1):
            yield (b, "keys", hp), (b, "query", c)
    for t in range(GATHERED[b], TT):
        yield (b, "chosen", t), None


JOB, CHUNKS, LAST_JOB = {}, [], {}
for _b in range(BATCHES):
    for _job, _chunk in jobs_of(_b):
        JOB[_job] = len(JOB)
        if _chunk is not None:
            if _chunk not in LAST_JOB:
                CHUNKS.append(_chunk)
            LAST_JOB[_chunk] = _job


def chunk_order(b):
    return [c for c in CHUNKS if c[0] == b]


def encoder_kernel(nc, x_prompt, x_sample, w_in, pool_w, w_pool_out, w_attn_out, w_out, w_query,
                   keysT, expert_u, expert_v, expert_uT, g_mix, pool_scale, q_norm, k_norm, g_ffn, g_final,
                   ident_c, band_c, rope_c, iota_c, y_prompt, y_sample):
    xs, ys = (x_prompt, x_sample), (y_prompt, y_sample)
    ctx = ExitStack()
    with ctx:
        def sb(name, shape, dt=F32):
            return ctx.enter_context(nc.sbuf_tensor(name, shape, dt))

        def sem(name):
            return ctx.enter_context(nc.semaphore(name))

        def sems(name, n):
            return [sem(f"{name}{i}") for i in range(n)]

        banks = [ctx.enter_context(nc.psum_tensor(f"bank{i}", [P, 512], F32)) for i in range(BANKS)]
        o_banks = [ctx.enter_context(nc.psum_tensor(f"o_bank{i}", [P, PAIRS, P], F32)) for i in range(2)]

        wslot = sb("wslot", [P, WSLOTS, KD * CHUNK])
        keys_sb = sb("keys_sb", [P, WSLOTS, 2 * N_KEYS])
        region_a = sb("region_a", [P, TT * D])
        region_b = sb("region_b", [P, TT * D])
        region_c = sb("region_c", [P, TT * D])
        h2 = sb("h2", [P, TT, D])
        ring = sb("ring", [P, RING, D])
        region_p = sb("region_p", [P, TT * POOL_W + GROUPS * T])
        region_q = sb("region_q", [P, TT * QKV_W + 2 * QK_HEADS * HD])
        region_s = sb("region_s", [P, 6 * T])
        gate_attn = sb("gate_attn", [P, 2, T])
        ident = sb("ident", [P, P])
        band = sb("band", [P, GROUPS, BAND_W])
        rope = sb("rope", [P, TT, 2, HD])
        iota = sb("iota", [P, P])
        pool_w_sb = sb("pool_w_sb", [P, GROUPS, P])
        g_mix_sb = sb("g_mix_sb", [P, KD])
        pool_scale_sb = sb("pool_scale_sb", [P, GROUPS])
        qk_norm_sb = sb("qk_norm_sb", [P, 2, HD])
        g_row = sb("g_row", [P, D])
        idx = sb("idx", [P, BATCHES, TT * SLOTS], U32)
        idx_now = sb("idx_now", [P, 2, RING], U32)
        gate = sb("gate", [P, BATCHES, TT, SLOTS])
        dots = sb("dots", [P, TT * SLOTS])
        dots_now = sb("dots_now", [P, BODY])
        stat = sb("stat", [P, 3, TT])
        head_stat = sb("head_stat", [P, TT, QK_HEADS])
        neg_max = sb("neg_max", [P, 2])
        prob_sum = sb("prob_sum", [P, 2])
        eps = sb("eps", [P, 1])

        xa = region_b[:, :].rearrange("p (t d) -> p t d", t=TT)
        hT = region_a[:, :].rearrange("p (k t) -> p k t", k=KD)
        gate_pool = region_b[:, :].rearrange("p (k t) -> p k t", k=KD)
        merged = gate_pool
        h2T = gate_pool
        x1s = [r[:, :].rearrange("p (t d) -> p t d", t=TT) for r in (region_c, region_a)]
        region_p0, region_p1 = region_p[:, 0:TT * POOL_W], region_p[:, TT * POOL_W:]
        pool_in = region_p0.rearrange("p (t c) -> p t c", t=TT)
        attnT = region_p0.rearrange("p (j t) -> p j t", j=PAIRS)
        pooledT = region_p1.rearrange("p (g t) -> p g t", g=GROUPS)
        qT = region_p1.rearrange("p (j t) -> p j t", j=PAIRS)
        qkv = region_q[:, 0:TT * QKV_W].rearrange("p (t n) -> p t n", t=TT)
        rope1 = region_q[:, TT * QKV_W:TT * QKV_W + QK_HEADS * HD]
        rope2 = region_q[:, TT * QKV_W + QK_HEADS * HD:]
        junk, last_junk = region_q[:, 0:D], region_p[:, 0:D]
        h2_to_turn = [h2, region_q[:, 0:TT * D].rearrange("p (t d) -> p t d", t=TT)]
        mixedT = region_s[:, 0:GROUPS * T].rearrange("p (g t) -> p g t", g=GROUPS)
        kT = region_s[:, 0:T]
        probs = region_s[:, T:3 * T].rearrange("p (a s) -> p a s", a=2)
        probsT = region_s[:, 3 * T:5 * T].rearrange("p (a s) -> p a s", a=2)
        peer_q = region_s[:, 0:2 * T].rearrange("p (a t) -> p a t", a=2)
        score = region_s[:, 2 * T:6 * T].rearrange("p (a t n) -> p a t n", a=4, t=TT)
        at = [0]

        def scratch(n):
            at[0] += n
            return region_q[:, at[0] - n:at[0]]

        best = scratch(TT * HALVES * TOPK).rearrange("p (t a k) -> p t a k", t=TT, a=HALVES)
        best_at = scratch(TT * HALVES * TOPK // 2).bitcast(mybir.dt.uint16).rearrange(
            "p (t a k) -> p t a k", t=TT, a=HALVES)
        sel_f = scratch(HALVES * TOPK).rearrange("p (a k) -> p a k", a=HALVES)
        cand = scratch(PEER_HEADS * CAND).rearrange("p (h n) -> p h n", h=PEER_HEADS)
        cand_id = scratch(PEER_HEADS * CAND).rearrange("p (h n) -> p h n", h=PEER_HEADS)
        match = scratch(TOPK * CAND)
        chosen = region_s[:, 0:3 * DENSE_T].rearrange("p (a t) -> p a t", a=3)
        parts = region_s[:, 3 * DENSE_T:5 * DENSE_T].rearrange("p (t a n) -> p t a n", t=DENSE, a=2)
        part_u = region_s[:, 5 * DENSE_T:5 * DENSE_T + SLOTS].bitcast(U32)
        one_hot_i = keys_sb[:, :, :].rearrange("p a (b n) -> p (a b) n", n=P)
        one_hot_j = gate_attn[:, :, :].rearrange("p a (b n) -> p (a b) n", n=P)
        blocks = [region_q[:, 0:N_KEYS * BLOCK], region_p[:, 0:N_KEYS * BLOCK]]
        weight_dram = nc.dram_tensor("expert_weights", (P, BLOCKS, N_KEYS, BLOCK), F32, kind="Internal").ap()
        u_cols = [wslot[:, n, 0:D].rearrange("p (k i) -> p k i", k=KD) for n in range(2)]
        v_cols = [wslot[:, 2 + n, 0:D] for n in range(2)]
        UNIT = 3 * DENSE_T
        weights_in = [region_s[:, n * UNIT:(n + 1) * UNIT] for n in range(2)]
        hidden = [region_q[:, n * DENSE_T:(n + 1) * DENSE_T] for n in range(2)]
        dense_out = banks
        dense_in = [o[:, :, :].rearrange("p a b -> p (a b)")
                    for o in o_banks]

        bank_filled, bank_freed = sems("bank_filled", BANKS), sems("bank_freed", BANKS)
        o_filled, o_freed = sems("o_filled", 2), sems("o_freed", 2)
        w_loaded = sems("w_loaded", WSLOTS)
        keys_loaded = sems("keys_loaded", WSLOTS)
        x_loaded = sems("x_loaded", TT)
        res_loaded = sem("res_loaded")
        first_loaded, consts_loaded = sem("first_loaded"), sem("consts_loaded")
        g_loaded = sem("g_loaded")
        act_step, dve_step = sem("act_step"), sem("dve_step")
        std_ready = sem("std_ready")
        xr_ready = sem("xr_ready")
        head_sq_ready, head_std_ready, roped = sem("head_sq_ready"), sem("head_std_ready"), sem("roped")
        pool_merged = sem("pool_merged")
        max_ready, exp_ready, probs_ready = sem("max_ready"), sem("exp_ready"), sem("probs_ready")
        merged_ready, x1_ready = sem("merged_ready"), sem("x1_ready")
        std2_ready, h2_ready = sem("std2_ready"), sem("h2_ready")
        halves_done = sem("halves_done")
        top_ready, top_exp = sem("top_ready"), sem("top_exp")
        idx_ready = sem("idx_ready")
        row_landed = sems("row_landed", RING)
        rows_used = sem("rows_used")
        idx_staged, slot_ok = sem("idx_staged"), sem("slot_ok")
        dots_saved, gelu_ready = sem("dots_saved"), sem("gelu_ready")
        parts_ready, one_hot_ready = sem("parts_ready"), sem("one_hot_ready")
        block_filled, block_freed = sems("block_filled", 2), sems("block_freed", 2)
        block_moved, block_stored = sem("block_moved"), sems("block_stored", 2)
        u_loaded, v_loaded, weights_loaded = sems("u_loaded", 2), sems("v_loaded", 2), sems("weights_loaded", 2)
        col_filled, col_moved = sem("col_filled"), sem("col_moved")
        hidden_ready, col_added = sem("hidden_ready"), sem("col_added")
        dense_added = sem("dense_added")
        std3_ready, y_ready, y_stored = sem("std3_ready"), sem("y_ready"), sem("y_stored")

        def filled(eng, *job):
            n = JOB[job]
            eng.wait_ge(bank_filled[n % BANKS], n // BANKS + 1)
            return banks[n % BANKS]

        def moved(eng, *job):
            n = JOB[job]
            eng.wait_ge(bank_freed[n % BANKS], n // BANKS + 1)

        def frees(*job):
            return bank_freed[JOB[job] % BANKS]

        block = ctx.enter_context(nc.Block())

        @block.sync
        def _(sp):
            def load_x(b):
                if b:
                    filled(sp, b - 1, "query", HALVES - 1)
                for t in range(TT):
                    sp.dma_start(xa[:, t, :], xs[b][0, t * P:(t + 1) * P, :]).then_inc(x_loaded[t], 16)

            def load_residual(b):
                if b:
                    filled(sp, b, "gate_attn", KD - 1)
                sp.dma_start(x1s[b], xs[b][0].rearrange("(t p) d -> p t d", p=P)).then_inc(res_loaded, 16)

            load_x(0)
            sp.dma_start(ident[:], ident_c).then_inc(first_loaded, 16)
            sp.dma_start(g_mix_sb[:], g_mix).then_inc(first_loaded, 16)

            w_in_cols = {"p": 0, "q": POOL_W, "kv": POOL_W + Q_W, "gate_pool": POOL_W + QKV_W,
                         "gate_attn": POOL_W + QKV_W + D}
            for b in range(BATCHES):
                if b:
                    load_x(b)
                for n, chunk in enumerate(chunk_order(b)):
                    m = CHUNKS.index(chunk)
                    if m >= WSLOTS:
                        filled(sp, *LAST_JOB[CHUNKS[m - WSLOTS]])
                    name, c = chunk[1], (chunk[2] if len(chunk) > 2 else 0)
                    dst = wslot[:, m % WSLOTS, :]
                    if name in w_in_cols:
                        at0 = w_in_cols[name] + c * CHUNK
                        src = w_in[:, at0:at0 + CHUNK].rearrange("(k p) n -> p k n", p=P)
                        dst = dst.rearrange("p (k n) -> p k n", k=KD)
                    elif name == "pool_out":
                        src = w_pool_out[:, c * 512:(c + 1) * 512].rearrange("(g p) n -> p g n", p=P)
                        dst = dst.rearrange("p (g n) -> p g n", g=GROUPS)
                    elif name == "attn_out":
                        dst = dst.rearrange("p (j n) -> p j n", j=PAIRS)
                        for half in range(KV_HEADS):
                            src = w_attn_out[half * PAIRS * HD:(half + 1) * PAIRS * HD,
                                             c * 512:(c + 1) * 512].rearrange("(j p) n -> p j n", p=HD)
                            sp.dma_start(dst[half * HD:(half + 1) * HD], src).then_inc(
                                w_loaded[m % WSLOTS], 16)
                        continue
                    else:
                        w = w_out if name == "out" else w_query
                        src = w[:, c * CHUNK:(c + 1) * CHUNK].rearrange("(k p) n -> p k n", p=P)
                        dst = dst.rearrange("p (k n) -> p k n", k=KD)
                    sp.dma_start(dst, src).then_inc(w_loaded[m % WSLOTS], 16)
                    if name == "query":
                        sp.dma_start(keys_sb[:, m % WSLOTS, :],
                                     keysT[:, c * 2 * N_KEYS:(c + 1) * 2 * N_KEYS]).then_inc(
                                         keys_loaded[m % WSLOTS], 16)
                    if b == 0 and n == 3:
                        sp.dma_start(rope[:], rope_c).then_inc(consts_loaded, 16)
                        sp.dma_start(qk_norm_sb[:, 0, :], q_norm.partition_broadcast(P)).then_inc(consts_loaded, 16)
                        sp.dma_start(qk_norm_sb[:, 1, :], k_norm.partition_broadcast(P)).then_inc(consts_loaded, 16)
                        sp.dma_start(band[:], band_c).then_inc(consts_loaded, 16)
                        sp.dma_start(pool_w_sb[:], pool_w.rearrange("g c d -> c g d")).then_inc(consts_loaded, 16)
                        sp.dma_start(pool_scale_sb[:], pool_scale).then_inc(consts_loaded, 16)
                        sp.dma_start(iota[:], iota_c).then_inc(consts_loaded, 16)
                        sp.dma_start(g_row[:], g_ffn.partition_broadcast(P)).then_inc(g_loaded, 16)
                    if name == "out" and c == 1:
                        load_residual(b)
            sp.wait_ge(h2_ready, BATCHES * TT)
            sp.dma_start(g_row[:], g_final.partition_broadcast(P)).then_inc(g_loaded, 16)

            for n in range(BLOCKS):
                sp.wait_ge(block_moved, 8 * (n + 1))
                sp.dma_start(weight_dram[:, n, :, :].rearrange("i j t -> i (j t)"),
                             blocks[n % 2]).then_inc(block_stored[n % 2], 16)
            for n in range(2):
                sp.wait_ge(block_stored[n], 16 * BLOCKS // 2)

            def load_column(j, q, waits):
                if waits:
                    sp.wait_ge(col_filled, j - 1)
                sp.dma_start(u_cols[q].rearrange("p k i -> p (k i)").unsqueeze(1),
                             expert_uT[:, bass.ds(j, 1), :]).then_inc(u_loaded[q], 16)
                if waits:
                    sp.wait_ge(col_added, j + 1)
                sp.dma_start(v_cols[q].unsqueeze(1),
                             expert_v.rearrange("(i j) d -> i j d", j=N_KEYS)[:, bass.ds(j, 1), :]).then_inc(
                                 v_loaded[q], 16)

            def load_weights(j, cols, u, waits):
                if waits:
                    sp.wait_ge(hidden_ready, j - cols)
                sp.dma_start(weights_in[u][:, 0:cols * DENSE_T].rearrange("p (b j t) -> p b j t", j=cols, t=BLOCK),
                             weight_dram[:, :, bass.ds(j, cols), :]).then_inc(weights_loaded[u], 16)

            first = True
            for key in COLS_BESIDE:
                cols = COLS_BESIDE[key] // 2
                count = GATHERED[key[0]] * SUBS
                j0 = COLS_START[key]

                def both(base, waits, waits_w):
                    for u in range(2):
                        load_weights(base + u * cols, cols, u, waits_w)
                        for c in range(cols):
                            q = (u * cols + c) % 2
                            load_column(base + u * cols + c, q, waits or u * cols + c >= 2)

                if first:
                    both(j0, False, False)
                    with sp.Fori(1, count) as i:
                        both(i * (2 * cols) + j0, True, True)
                else:
                    sp.wait_ge(hidden_ready, j0)
                    with sp.Fori(0, count) as i:
                        both(i * (2 * cols) + j0, True, True)
                first = False

        FIRST_ALL, CONSTS_ALL = 2 * 16, 7 * 16

        def chunk_landed(eng, chunk):
            m = CHUNKS.index(chunk)
            count = 0
            for n in range(m % WSLOTS, m + 1, WSLOTS):
                count += 2 if CHUNKS[n][1] == "attn_out" else 1
            eng.wait_ge(w_loaded[m % WSLOTS], 16 * count)
            return m % WSLOTS

        @block.tensor
        def _(pe):
            def fill(*job):
                n = JOB[job]
                if n >= BANKS:
                    pe.wait_ge(bank_freed[n % BANKS], n // BANKS)
                return banks[n % BANKS]

            def done(ins, *job):
                ins.then_inc(bank_filled[JOB[job] % BANKS], 1)

            def turned(job, src):
                bank = fill(*job)
                for t in range(TT):
                    ins = nc.tensor.transpose(bank[:, t * P:(t + 1) * P], src(t), ident[:])
                done(ins, *job)

            def token_major(job, chunk, lhs, tp):
                slot = chunk_landed(pe, chunk)
                w = wslot[:, slot, :].rearrange("p (k n) -> p k n", k=KD)
                bank = fill(*job)
                for tt in range(2):
                    t = 2 * tp + tt
                    for k in range(KD):
                        ins = nc.tensor.matmul(bank[:, tt * CHUNK:(tt + 1) * CHUNK],
                                               lhs[:, k, t * P:(t + 1) * P], w[:, k, :],
                                               start=(k == 0), stop=(k == KD - 1))
                done(ins, *job)

            def feature_major(job, chunk, rhs, col, steps):
                slot = chunk_landed(pe, chunk)
                w = wslot[:, slot, :].rearrange("p (k n) -> p k n", k=steps)
                bank = fill(*job)
                for k in range(steps):
                    ins = nc.tensor.matmul(bank[:], w[:, k, col:col + P], rhs[:, k, :],
                                           start=(k == 0), stop=(k == steps - 1))
                done(ins, *job)

            steps = attention_steps()
            for b in range(BATCHES):
                if b == 0:
                    pe.wait_ge(first_loaded, FIRST_ALL)
                for k in range(KD):
                    if k == 0:
                        pe.wait_ge(xr_ready, TT * (b + 1))
                    turned((b, "hT", k), lambda t: xa[:, t, k * P:(k + 1) * P])
                for k in range(KD):
                    moved(pe, b, "hT", k)
                for c in range(2):
                    for tp in range(2):
                        token_major((b, "q", c, tp), (b, "q", c), hT, tp)
                for tp in range(2):
                    token_major((b, "kv", tp), (b, "kv"), hT, tp)
                for c in range(2):
                    for tp in range(2):
                        token_major((b, "p", c, tp), (b, "p", c), hT, tp)
                if b == 0:
                    pe.wait_ge(consts_loaded, CONSTS_ALL)
                for g in range(GROUPS):
                    for tp in range(2):
                        moved(pe, b, "p", g // 2, tp)
                    bank = fill(b, "pooled", g)
                    for t in range(TT):
                        cols = slice(g * P, (g + 1) * P)
                        kind = 0 if t == 0 else (2 if t == TT - 1 else 1)
                        ins = nc.tensor.matmul(bank[:, t * P:(t + 1) * P], pool_in[:, t, cols],
                                               band[:, g, kind * P:(kind + 1) * P], start=True,
                                               stop=False, skip_group_check=True)
                        if t > 0:
                            ins = nc.tensor.matmul(bank[:, t * P:t * P + EDGE], pool_in[:, t - 1, cols],
                                                   band[:, g, 3 * P:3 * P + EDGE], start=False,
                                                   stop=(t == TT - 1), skip_group_check=True)
                        if t < TT - 1:
                            ins = nc.tensor.matmul(bank[:, (t + 1) * P - EDGE:(t + 1) * P],
                                                   pool_in[:, t + 1, cols],
                                                   band[:, g, 3 * P + EDGE:], start=False,
                                                   stop=True, skip_group_check=True)
                    done(ins, b, "pooled", g)
                for g in range(GROUPS):
                    moved(pe, b, "pooled", g)
                    bank = fill(b, "mixed", g)
                    ins = nc.tensor.matmul(bank[:], pool_w_sb[:, g, :], pooledT[:, g, :], start=True, stop=True)
                    done(ins, b, "mixed", g)
                for d in range(KD):
                    feature_major((b, "gate_pool", d), (b, "gate_pool", d // 2), hT, d % 2 * P, KD)
                for g in range(GROUPS):
                    moved(pe, b, "mixed", g)
                for d in range(KD):
                    feature_major((b, "pool_out", d), (b, "pool_out", d // 4), mixedT, d % 4 * P, GROUPS)
                pe.wait_ge(roped, TT * (b + 1))
                for j in range(PAIRS):
                    turned((b, "qT", j), lambda t: qkv[:, t, j * P:(j + 1) * P])
                turned((b, "kT"), lambda t: qkv[:, t, Q_W:Q_W + KV_W])

                def scores(i):
                    t, j, half = steps[i]
                    if i == 0:
                        moved(pe, b, "kT")
                        for jj in range(PAIRS):
                            moved(pe, b, "qT", jj)
                    bank = fill(b, "s", i)
                    rows = slice(half * HD, (half + 1) * HD)
                    ins = nc.tensor.matmul(bank[:], qT[rows, j, t * P:(t + 1) * P], kT[rows, :],
                                           start=True, stop=True)
                    done(ins, b, "s", i)

                def values(i):
                    t, j, half = steps[i]
                    if j == 0 and half == 0 and b * TT + t >= 2:
                        pe.wait_ge(o_freed[t % 2], (b * TT + t) // 2)
                    moved(pe, b, "probsT", i)
                    for s in range(TT):
                        v = qkv[:, s, Q_W + KV_W + half * HD:Q_W + KV_W + (half + 1) * HD]
                        ins = nc.tensor.matmul(o_banks[t % 2][half * HD:(half + 1) * HD, j, :], v,
                                               probsT[:, i % 2, s * P:(s + 1) * P],
                                               start=(s == 0), stop=(s == TT - 1))
                    if j == PAIRS - 1 and half == 1:
                        ins.then_inc(o_filled[t % 2], 1)

                scores(0)
                scores(1)
                for i in range(len(steps)):
                    if i + 2 < len(steps):
                        scores(i + 2)
                    pe.wait_ge(probs_ready, b * len(steps) + i + 1)
                    turned((b, "probsT", i), lambda s: probs[:, i % 2, s * P:(s + 1) * P])
                    if i:
                        values(i - 1)
                values(len(steps) - 1)
                for c in range(KD // 2):
                    for d in (2 * c, 2 * c + 1):
                        feature_major((b, "gate_attn", d), (b, "gate_attn", c), hT, d % 2 * P, KD)
                    if c == 0:
                        for t in range(2):
                            pe.wait_ge(o_freed[t], (b + 1) * TT // 2)
                    for d in (2 * c, 2 * c + 1):
                        feature_major((b, "attn_out", d), (b, "attn_out", d // 4), attnT, d % 4 * P, PAIRS)
                pe.wait_ge(merged_ready, KD * (b + 1))
                for c in range(D // CHUNK):
                    for tp in range(2):
                        token_major((b, "out", c, tp), (b, "out", c), merged, tp)
                pe.wait_ge(h2_ready, TT * (b + 1))
                for k in range(KD):
                    turned((b, "h2T", k), lambda t: h2_to_turn[b][:, t, k * P:(k + 1) * P])
                for k in range(KD):
                    moved(pe, b, "h2T", k)
                for c in range(HALVES // 2):
                    for hp in (2 * c, 2 * c + 1):
                        feature_major((b, "query", hp), (b, "query", c), h2T, hp % 2 * P, KD)
                    m = CHUNKS.index((b, "query", c))
                    pe.wait_ge(keys_loaded[m % WSLOTS],
                               16 * sum(CHUNKS[n][1] == "query" for n in range(m % WSLOTS, m + 1, WSLOTS)))
                    for hp in (2 * c, 2 * c + 1):
                        moved(pe, b, "query", hp)
                        bank = fill(b, "keys", hp)
                        for t in range(TT):
                            ins = nc.tensor.matmul(bank[:, t * P:(t + 1) * P],
                                                   peer_q[:, hp % 2, t * P:(t + 1) * P],
                                                   keys_sb[:, m % WSLOTS, hp % 2 * N_KEYS:(hp % 2 + 1) * N_KEYS],
                                                   start=True, stop=True)
                        done(ins, b, "keys", hp)

            b = 1
            for t in range(GATHERED[b], TT):
                pe.wait_ge(parts_ready, t - GATHERED[b] + 1)
                bank = fill(b, "chosen", t)
                for a, src in enumerate((parts[:, t - GATHERED[b], 0, :], parts[:, t - GATHERED[b], 1, :],
                                         gate[:, b, t, :])):
                    ins = nc.tensor.transpose(bank[:, a * P:(a + 1) * P], src, ident[:])
                done(ins, b, "chosen", t)
            for n in range(2):
                pe.sem_inc(block_filled[n], 1)
            pe.sem_inc(col_added, 2)
            with pe.Fori(0, DENSE_T // OH_RING) as i:
                for r in range(OH_RING):
                    pe.wait_ge(one_hot_ready, i * OH_RING + r + 1)
                    if r % 4 == 0:
                        pe.wait_ge(block_freed[r // 4], i + 1)
                    ins = nc.tensor.matmul(dense_in[r // 4][:, r % 4 * P:(r % 4 + 1) * P], one_hot_i[:, r, :],
                                           one_hot_j[:, r, :], start=True, stop=True)
                    if r % 4 == 3:
                        ins.then_inc(block_filled[r // 4], 1)

            def take_column(j, q, turn):
                pe.wait_ge(u_loaded[q], turn * 16)
                if isinstance(j, int) and j < 2:
                    for n in range(2):
                        pe.wait_ge(block_freed[n], DENSE_T // OH_RING + 1)
                else:
                    pe.wait_ge(col_moved, j - 1)
                for k in range(KD):
                    ins = nc.tensor.matmul(dense_in[q][:, 0:DENSE_T], u_cols[q][:, k, :],
                                           h2T[:, k, T - DENSE_T:T], start=(k == 0), stop=(k == KD - 1))
                ins.then_inc(col_filled, 1)

            def add_column(j, q, turn, start=False, stop=False):
                pe.wait_ge(v_loaded[q], turn * 16)
                pe.wait_ge(hidden_ready, j + 1)
                for t in range(DENSE):
                    for n in range(2):
                        ins = nc.tensor.matmul(dense_out[2 * t + n][:], hidden[q][:, t * P:(t + 1) * P],
                                               v_cols[q][:, n * 512:(n + 1) * 512], start=start, stop=stop,
                                               skip_group_check=True)
                ins.then_inc(col_added, 1)

            take_column(0, 0, 1)
            take_column(1, 1, 1)
            for t in range(GATHERED[b], TT):
                moved(pe, b, "chosen", t)
            add_column(0, 0, 1, start=True)
            with pe.Fori(0, (N_KEYS - 2) // 2) as i:
                take_column(i * 2 + 2, 0, i + 2)
                add_column(i * 2 + 1, 1, i + 1)
                take_column(i * 2 + 3, 1, i + 2)
                add_column(i * 2 + 2, 0, i + 2)
            add_column(N_KEYS - 1, 1, N_KEYS // 2, stop=True)

        @block.scalar
        def _(act):
            n_act = [0]

            def link(ins):
                n_act[0] += 1
                ins.then_inc(act_step, 1)
                act.wait_ge(act_step, n_act[0])

            def move(dst, job, func=ACT.Identity, scale=1.0, view=None):
                bank = filled(act, *job)
                src = bank[:] if view is None else view(bank)
                nc.scalar.activation(dst, src, func, scale=scale).then_inc(frees(*job), 1)

            def norm1(b):
                if b:
                    act.wait_ge(idx_ready, TT * b)
                for t in range(TT):
                    act.wait_ge(x_loaded[t], 16 * (b + 1))
                    link(nc.scalar.activation(junk, xa[:, t, :], ACT.Square, accum_out=stat[:, 0, t:t + 1]))
                nc.scalar.activation(stat[:, 0, :], stat[:, 0, :], ACT.Sqrt, bias=eps[:],
                                     scale=1.0 / D).then_inc(std_ready, 1)

            def projections(b):
                if b == 0:
                    act.wait_ge(first_loaded, FIRST_ALL)
                for k in range(KD):
                    move(hT[:, k, :], (b, "hT", k), scale=g_mix_sb[:, k:k + 1])
                pair = lambda bank: bank[:].rearrange("p (t n) -> p t n", t=2)
                for c in range(2):
                    for tp in range(2):
                        move(qkv[:, 2 * tp:2 * tp + 2, c * CHUNK:(c + 1) * CHUNK], (b, "q", c, tp), view=pair)
                for tp in range(2):
                    move(qkv[:, 2 * tp:2 * tp + 2, Q_W:QKV_W], (b, "kv", tp), view=pair)
                for c in range(2):
                    for tp in range(2):
                        move(pool_in[:, 2 * tp:2 * tp + 2, c * CHUNK:(c + 1) * CHUNK], (b, "p", c, tp), view=pair)
                act.wait_ge(head_sq_ready, b + 1)
                nc.scalar.activation(head_stat[:], head_stat[:], ACT.Sqrt, bias=eps[:],
                                     scale=1.0 / HD).then_inc(head_std_ready, 1)
                for g in range(GROUPS):
                    move(pooledT[:, g, :], (b, "pooled", g))
                if b == 0:
                    act.wait_ge(consts_loaded, CONSTS_ALL)
                for g in range(GROUPS):
                    move(mixedT[:, g, :], (b, "mixed", g), scale=pool_scale_sb[:, g:g + 1])
                for d in range(KD):
                    move(gate_pool[:, d, :], (b, "gate_pool", d), ACT.Sigmoid)

            def attention(b):
                n = len(attention_steps())
                for j in range(PAIRS):
                    move(qT[:, j, :], (b, "qT", j), scale=HD ** -0.5)
                move(kT, (b, "kT"))

                def exp(i):
                    bank = filled(act, b, "s", i)
                    act.wait_ge(max_ready, b * n + i + 1)
                    if i >= 2:
                        filled(act, b, "probsT", i - 2)
                    nc.scalar.activation(probs[:, i % 2, :], bank[:], ACT.Exp, bias=neg_max[:, i % 2:i % 2 + 1],
                                         accum_out=prob_sum[:, i % 2:i % 2 + 1]).then_inc(exp_ready, 1)

                exp(0)
                for i in range(n):
                    if i + 1 < n:
                        exp(i + 1)
                    move(probsT[:, i % 2, :], (b, "probsT", i))
                    if i % HEADS == 0 and i:
                        outputs(b, i // HEADS - 1)
                outputs(b, TT - 1)

            def outputs(b, t):
                act.wait_ge(o_filled[t % 2], (b * TT + t) // 2 + 1)
                nc.scalar.activation(attnT[:, :, t * P:(t + 1) * P], o_banks[t % 2][:],
                                     ACT.Identity).then_inc(o_freed[t % 2], 1)

            def gates(b):
                for d in range(KD):
                    if d >= 2:
                        act.wait_ge(merged_ready, b * KD + d - 1)
                    move(gate_attn[:, d % 2, :], (b, "gate_attn", d), ACT.Sigmoid)

            def norm2(b):
                for t in range(TT):
                    act.wait_ge(x1_ready, b * 8 + 8)
                    link(nc.scalar.activation(junk, x1s[b][:, t, :], ACT.Square, accum_out=stat[:, 1, t:t + 1]))
                nc.scalar.activation(stat[:, 1, :], stat[:, 1, :], ACT.Sqrt, bias=eps[:],
                                     scale=1.0 / D).then_inc(std2_ready, 1)

            def queries(b):
                for k in range(KD):
                    move(h2T[:, k, :], (b, "h2T", k))
                for c in range(HALVES // 2):
                    for hp in (2 * c, 2 * c + 1):
                        move(peer_q[:, hp % 2, :], (b, "query", hp))
                    for hp in (2 * c, 2 * c + 1):
                        if hp >= 4:
                            act.wait_ge(halves_done, b * HALVES + hp - 3)
                        move(score[:, hp % 4, :, :], (b, "keys", hp),
                             view=lambda bank: bank[:].rearrange("p (t n) -> p t n", t=TT))

            def gate_exp(b, t):
                act.wait_ge(top_ready, b * TT + t + 1)
                g = gate[:, b, t, :]
                nc.scalar.activation(g, g, ACT.Exp).then_inc(top_exp, 1)

            def gelu(b):
                act.wait_ge(dots_saved, sum(GATHERED[:b + 1]) * SLOTS // BODY)
                d = dots[:, 0:GATHERED[b] * SLOTS]
                nc.scalar.activation(d, d, ACT.Gelu).then_inc(gelu_ready, 1)

            def store_weights():
                for t in range(GATHERED[1], TT):
                    c = chosen[:, :, (t - GATHERED[1]) * P:(t - GATHERED[1] + 1) * P]
                    move(c, (1, "chosen", t), view=lambda bank: bank[:, 0:3 * P].rearrange("p (a t) -> p a t", a=3))
                for n in range(2):
                    act.sem_inc(block_freed[n], 1)

                def pair(turn, stored):
                    for n in range(2):
                        if stored is not None:
                            act.wait_ge(block_stored[n], stored)
                        dst = blocks[n].rearrange("p (j t) -> p t j", t=BLOCK)
                        for q in range(BLOCK // 4):
                            act.wait_ge(block_filled[q % 2], turn + (n * BLOCK // 8 + q // 2 + 2))
                            nc.scalar.activation(dst[:, 4 * q:4 * q + 4, :],
                                                 dense_in[q % 2].rearrange("p (t j) -> p t j", t=4),
                                                 ACT.Identity).then_inc(block_freed[q % 2], 1)
                            act.wait_ge(block_freed[q % 2], turn + (n * BLOCK // 8 + q // 2 + 2))
                            act.sem_inc(block_moved, 1)

                pair(0, None)
                with act.Fori(1, BLOCKS // 2) as i:
                    pair(i * (2 * BLOCK // 8), i * 16)

            def hidden_columns(first, count):
                with act.Fori(0, count // 2) as i:
                    for q in range(2):
                        j = i * 2 + (first + q)
                        act.wait_ge(col_filled, j + 1)
                        act.wait_ge(col_added, j + 1)
                        nc.scalar.activation(hidden[q], dense_in[q][:, 0:DENSE_T], ACT.Gelu).then_inc(col_moved, 1)

            def finish(b, t):
                if t < GATHERED[b]:
                    act.wait_ge(rows_used, RING + PHASE_START[b, 1] + (t + 1) * SLOTS)
                else:
                    act.wait_ge(dense_added, t - GATHERED[b] + 1)
                link(nc.scalar.activation(last_junk, x1s[b][:, t, :], ACT.Square, accum_out=stat[:, 2, t:t + 1]))
                nc.scalar.activation(stat[:, 2, t:t + 1], stat[:, 2, t:t + 1], ACT.Sqrt, bias=eps[:],
                                     scale=1.0 / D).then_inc(std3_ready, 1)
                act.wait_ge(y_ready, b * TT + t + 1)
                act.dma_start(ys[b][0, t * P:(t + 1) * P, :], x1s[b][:, t, :]).then_inc(y_stored, 16)

            act.wait_ge(dve_step, 1)
            norm1(0)
            projections(0)
            attention(0)
            gates(0)
            norm2(0)
            queries(0)
            for t in range(TT):
                gate_exp(0, t)
            norm1(1)
            projections(1)
            attention(1)
            gates(1)
            norm2(1)
            queries(1)
            for t in range(TT):
                gate_exp(1, t)
            store_weights()
            gelu(0)
            for n in range(2):
                act.wait_ge(block_stored[n], 16 * BLOCKS // 2)
            hidden_columns(0, COLS_START[1, 0])
            for t in range(TT):
                finish(0, t)
            hidden_columns(COLS_START[1, 0], COLS_START[1, 1] - COLS_START[1, 0])
            gelu(1)
            hidden_columns(COLS_START[1, 1], N_KEYS - COLS_START[1, 1])
            for t in range(TT):
                finish(1, t)
            act.wait_ge(y_stored, 16 * BATCHES * TT)

        @block.gpsimd
        def _(pool):
            for b in range(BATCHES):
                for phase, table in enumerate((expert_u, expert_v)):
                    base = PHASE_START[b, phase]
                    for t in range(GATHERED[b]):
                        pool.wait_ge(idx_ready, b * TT + t + 1)
                        with pool.Fori(0, SLOTS // BODY) as i:
                            for half in range(2):
                                n0 = i * BODY + base + t * SLOTS + half * RING
                                pool.wait_ge(rows_used, n0 + 1)
                                pool.sem_inc(slot_ok, 1)
                                nc.gpsimd.tensor_copy(
                                    idx_now[:, half, :],
                                    idx[:, b, bass.ds(i * BODY + t * SLOTS + half * RING, RING)]).then_inc(idx_staged, 1)
                                pool.wait_ge(idx_staged, (i * 2 + half + 1) + (base + t * SLOTS) // RING)
                                for r in range(RING):
                                    pool.wait_ge(rows_used, n0 + r + 1)
                                    pool.sem_inc(slot_ok, 1)
                                    nc.gpsimd.indirect_dma_start(
                                        ring[:, r, :], None, table,
                                        bass.IndirectOffsetOnAxis(ap=idx_now[:, half, r:r + 1], axis=0)).then_inc(row_landed[r], 16)

        @block.vector
        def _(dve):
            n_dve = [0]

            def step(ins):
                n_dve[0] += 1
                ins.then_inc(dve_step, 1)

            def sync():
                dve.wait_ge(dve_step, n_dve[0])

            def link(ins):
                step(ins)
                sync()

            def norm1(b):
                dve.wait_ge(std_ready, b + 1)
                link(nc.vector.reciprocal(stat[:, 0, :], stat[:, 0, :]))
                for t in range(TT):
                    nc.vector.tensor_scalar(xa[:, t, :], xa[:, t, :], stat[:, 0, t:t + 1], None,
                                            ALU.mult).then_inc(xr_ready, 1)

            def rotate(b):
                if b == 0:
                    dve.wait_ge(consts_loaded, CONSTS_ALL)
                for t in range(TT):
                    if t % 2 == 0:
                        for c in range(2):
                            moved(dve, b, "q", c, t // 2)
                        moved(dve, b, "kv", t // 2)
                    qk = qkv[:, t, 0:Q_W + KV_W]
                    link(nc.vector.tensor_tensor(rope1, qk, qk, ALU.mult))
                    link(nc.vector.tensor_reduce(head_stat[:, t, :], rope1.rearrange("p (h d) -> p h d", d=HD),
                                                 AX.X, ALU.add))
                dve.sem_inc(head_sq_ready, 1)
                dve.wait_ge(head_std_ready, b + 1)
                link(nc.vector.reciprocal(head_stat[:], head_stat[:]))
                for t in range(TT):
                    heads = qkv[:, t, 0:Q_W + KV_W].rearrange("p (h d) -> p h d", d=HD)
                    r1, r2 = (r.rearrange("p (h d) -> p h d", d=HD) for r in (rope1, rope2))
                    link(nc.vector.tensor_tensor(r1, heads, head_stat[:, t, :].unsqueeze(2).to_broadcast(
                        [P, QK_HEADS, HD]), ALU.mult))
                    step(nc.vector.tensor_tensor(heads[:, 0:HEADS, :], r1[:, 0:HEADS, :],
                                                 qk_norm_sb[:, 0:1, :].to_broadcast([P, HEADS, HD]), ALU.mult))
                    link(nc.vector.tensor_tensor(heads[:, HEADS:, :], r1[:, HEADS:, :],
                                                 qk_norm_sb[:, 1:2, :].to_broadcast([P, KV_HEADS, HD]), ALU.mult))
                    step(nc.vector.tensor_tensor(r1, heads, rope[:, t, 0:1, :].to_broadcast([P, QK_HEADS, HD]),
                                                 ALU.mult))
                    for q in range(2):
                        src = heads.rearrange("p h (a q d) -> p h a q d", a=2, q=2)[:, :, :, 1 - q, :]
                        dst = r2.rearrange("p h (a q d) -> p h a q d", a=2, q=2)[:, :, :, q, :]
                        sin = rope[:, t, 1:2, :].rearrange("p o (a q d) -> p o a q d", a=2, q=2)[:, :, :, q, :]
                        step(nc.vector.tensor_tensor(dst, src, sin.to_broadcast([P, QK_HEADS, 2, HD // 4]), ALU.mult))
                    sync()
                    pairs = qkv[:, t, 0:Q_W].rearrange("p (j a d) -> p a j d", j=PAIRS, d=HD)
                    for half in range(KV_HEADS):
                        hs = slice(half * PAIRS, (half + 1) * PAIRS)
                        step(nc.vector.tensor_tensor(pairs[:, half], r1[:, hs, :], r2[:, hs, :], ALU.add))
                    link(nc.vector.tensor_tensor(heads[:, HEADS:, :], r1[:, HEADS:, :], r2[:, HEADS:, :], ALU.add))
                    dve.sem_inc(roped, 1)

            def pool_out(b):
                for d in range(KD):
                    bank = filled(dve, b, "pool_out", d)
                    nc.vector.tensor_tensor(merged[:, d, :], gate_pool[:, d, :], bank[:],
                                            ALU.mult).then_inc(frees(b, "pool_out", d), 1)

            n_att = len(attention_steps())

            def row_max(b, i):
                bank = filled(dve, b, "s", i)
                if i >= 2:
                    dve.wait_ge(exp_ready, b * n_att + i - 1)
                nc.vector.tensor_reduce(neg_max[:, i % 2:i % 2 + 1], bank[:], AX.X, ALU.max,
                                        negate=True).then_inc(max_ready, 1)

            def normalise(b, i):
                dve.wait_ge(exp_ready, b * n_att + i + 1)
                link_free = nc.vector.reciprocal(prob_sum[:, i % 2:i % 2 + 1], prob_sum[:, i % 2:i % 2 + 1])
                link_free.then_inc(frees(b, "s", i), 1)
                moved(dve, b, "s", i)
                nc.vector.tensor_scalar(probs[:, i % 2, :], probs[:, i % 2, :], prob_sum[:, i % 2:i % 2 + 1],
                                        None, ALU.mult).then_inc(probs_ready, 1)

            def attention(b, first, last):
                if first == 0:
                    row_max(b, 0)
                for i in range(first, last):
                    if i + 1 < n_att:
                        row_max(b, i + 1)
                    normalise(b, i)

            def attn_out(b, first, last):
                for d in range(first, last):
                    moved(dve, b, "gate_attn", d)
                    bank = filled(dve, b, "attn_out", d)
                    g = gate_attn[:, d % 2, :]
                    nc.vector.tensor_tensor(g, g, bank[:], ALU.mult).then_inc(frees(b, "attn_out", d), 1)
                    moved(dve, b, "attn_out", d)
                    nc.vector.tensor_tensor(merged[:, d, :], merged[:, d, :], g, ALU.add).then_inc(merged_ready, 1)

            def out(b):
                dve.wait_ge(res_loaded, 16 * (b + 1))
                for c in range(D // CHUNK):
                    for tp in range(2):
                        bank = filled(dve, b, "out", c, tp)
                        x = x1s[b][:, 2 * tp:2 * tp + 2, c * CHUNK:(c + 1) * CHUNK]
                        ins = nc.vector.tensor_tensor(x, x, bank[:].rearrange("p (t n) -> p t n", t=2), ALU.add)
                        ins.then_inc(frees(b, "out", c, tp), 1)
                for c in range(D // CHUNK):
                    for tp in range(2):
                        moved(dve, b, "out", c, tp)
                dve.sem_inc(x1_ready, 8)

            def norm2(b):
                if b == 0:
                    dve.wait_ge(g_loaded, 16)
                dve.wait_ge(std2_ready, b + 1)
                link(nc.vector.reciprocal(stat[:, 1, :], stat[:, 1, :]))
                for t in range(TT):
                    nc.vector.scalar_tensor_tensor(out=h2_to_turn[b][:, t, :], in0=x1s[b][:, t, :],
                                                   scalar=stat[:, 1, t:t + 1], in1=g_row[:], op0=ALU.mult,
                                                   op1=ALU.mult).then_inc(h2_ready, 1)
                if b:
                    dve.wait_ge(h2_ready, TT * (b + 1))
                    for t in range(GATHERED[b]):
                        link(nc.vector.tensor_copy(h2[:, t, :], h2_to_turn[b][:, t, :]))

            def top_halves(b, hp):
                moved(dve, b, "keys", hp)
                s = score[:, hp % 4]
                for t in range(TT):
                    step(nc.vector.max(best[:, t, hp, 0:8], s[:, t, :]))
                sync()
                for t in range(TT):
                    step(nc.vector.max_index(best_at[:, t, hp, 0:8], best[:, t, hp, 0:8], s[:, t, :]))
                sync()
                for t in range(TT):
                    step(nc.vector.match_replace(s[:, t, :], best[:, t, hp, 0:8], s[:, t, :], LOWEST))
                sync()
                for t in range(TT):
                    step(nc.vector.max(best[:, t, hp, 8:16], s[:, t, :]))
                sync()
                for t in range(TT):
                    ins = nc.vector.max_index(best_at[:, t, hp, 8:16], best[:, t, hp, 8:16], s[:, t, :])
                ins.then_inc(halves_done, 1)

            def candidates(out, first, second):
                for a, rows, cols, off in CAND_RUNS:
                    dst = out[:, :, off:off + rows * cols]
                    left, right = first[:, :, a:a + rows], second[:, :, 0:cols]
                    if cols == 1:
                        right = right.to_broadcast([P, PEER_HEADS, rows])
                    elif rows == 1:
                        left = left.to_broadcast([P, PEER_HEADS, cols])
                    else:
                        dst = dst.rearrange("p h (a b) -> p h a b", b=cols)
                        left = left.unsqueeze(3).to_broadcast([P, PEER_HEADS, rows, cols])
                        right = right.unsqueeze(2).to_broadcast([P, PEER_HEADS, rows, cols])
                    step(nc.vector.tensor_tensor(dst, left, right, ALU.add))

            def merge(b, t):
                if t == 0:
                    dve.wait_ge(halves_done, HALVES * (b + 1))
                ids = sel_f
                view = best_at[:, t].rearrange("p (h a) k -> p h a k", a=2)
                idv = ids.rearrange("p (h a) k -> p h a k", a=2)
                val = best[:, t].rearrange("p (h a) k -> p h a k", a=2)
                step(nc.vector.tensor_scalar(idv[:, :, 0, :], view[:, :, 0, :], float(N_KEYS), None, ALU.mult))
                step(nc.vector.tensor_copy(idv[:, :, 1, :], view[:, :, 1, :]))
                candidates(cand, val[:, :, 0, :], val[:, :, 1, :])
                sync()
                candidates(cand_id, idv[:, :, 0, :], idv[:, :, 1, :])
                top = gate[:, b, t, :].rearrange("p (h k) -> p h k", k=TOPK)
                pos_i = best_at[:, t].rearrange("p (a h) k -> p a h k", a=2)[:, 0]
                for h in range(PEER_HEADS):
                    step(nc.vector.max(top[:, h, 0:8], cand[:, h, :]))
                sync()
                for h in range(PEER_HEADS):
                    step(nc.vector.max_index(pos_i[:, h, 0:8], top[:, h, 0:8], cand[:, h, :]))
                sync()
                for h in range(PEER_HEADS):
                    step(nc.vector.match_replace(cand[:, h, :], top[:, h, 0:8], cand[:, h, :], LOWEST))
                sync()
                for h in range(PEER_HEADS):
                    step(nc.vector.max(top[:, h, 8:16], cand[:, h, :]))
                sync()
                for h in range(PEER_HEADS):
                    step(nc.vector.max_index(pos_i[:, h, 8:16], top[:, h, 8:16], cand[:, h, :]))
                sync()
                pos = sel_f[:, 0:PEER_HEADS, :]
                found = sel_f[:, PEER_HEADS:, :]
                link(nc.vector.tensor_copy(pos, pos_i))
                for h in range(PEER_HEADS):
                    hit = match.rearrange("p (k n) -> p k n", n=CAND)
                    link(nc.vector.tensor_tensor(hit, pos[:, h, :].unsqueeze(2).to_broadcast([P, TOPK, CAND]),
                                                 iota[:, 0:CAND].unsqueeze(1).to_broadcast([P, TOPK, CAND]), ALU.is_equal))
                    link(nc.vector.tensor_tensor(hit, hit, cand_id[:, h:h + 1, :].to_broadcast([P, TOPK, CAND]),
                                                 ALU.mult))
                    link(nc.vector.tensor_reduce(found[:, h, :], hit, AX.X, ALU.add))
                nc.vector.tensor_copy(idx[:, b, t * SLOTS:(t + 1) * SLOTS].rearrange("p (h k) -> p h k", k=TOPK),
                                      found).then_inc(idx_ready, 1)
                link(nc.vector.tensor_copy(cand[:, :, 0:1], top[:, :, 0:1]))
                nc.vector.tensor_tensor(top, top, cand[:, :, 0:1].to_broadcast([P, PEER_HEADS, TOPK]),
                                        ALU.subtract).then_inc(top_ready, 1)
                dve.wait_ge(top_exp, b * TT + t + 1)
                link(nc.vector.tensor_reduce(cand[:, :, 0], top, AX.X, ALU.add))
                link(nc.vector.reciprocal(cand[:, :, 0], cand[:, :, 0]))
                link(nc.vector.tensor_tensor(top, top, cand[:, :, 0:1].to_broadcast([P, PEER_HEADS, TOPK]), ALU.mult))

            def weigh_column(j, cols, u, c):
                q = (u * cols + c) % 2
                dve.wait_ge(col_moved, j + 1)
                w = weights_in[u][:, 0:cols * DENSE_T].rearrange("p (b j t) -> p b j t", j=cols, t=BLOCK)
                h = hidden[q].rearrange("p (b t) -> p b t", t=BLOCK)
                nc.vector.tensor_tensor(h, h, w[:, :, c, :], ALU.mult).then_inc(hidden_ready, 1)

            def rows_and_columns(b, phase, t, i, take_row, first=0):
                start = PHASE_START[b, phase] + t * SLOTS + first * SUB
                beside = COLS_BESIDE.get((b, phase), 0)
                for s in range(SUB):
                    r = s % RING
                    dve.wait_ge(row_landed[r], (i * (SUB // RING) + (start // RING + s // RING + 1)) * 16)
                    take_row(i, s, r, start)
                    if beside and (s + 1) * beside // SUB > s * beside // SUB:
                        n = s * beside // SUB
                        cols = beside // 2
                        j = i * beside + (COLS_START[b, phase] + t * SUBS * beside + n)
                        if n % cols == 0:
                            before = UNITS_BEFORE[b, phase] + t * SUBS
                            dve.wait_ge(weights_loaded[n // cols], (i + (before + 1)) * 16)
                        weigh_column(j, cols, n // cols, n % cols)

            UNITS_BEFORE = {(0, 1): 0, (1, 0): GATHERED[0] * SUBS,
                            (1, 1): GATHERED[0] * SUBS + GATHERED[1] * SUBS}

            def dot_rows(b, t, first, count):
                dots_before = b * GATHERED[0] * SLOTS // BODY + (t * SLOTS + first * SUB) // BODY

                def take(i, s, r, start):
                    nc.vector.tensor_tensor_reduce(ring[:, r, :], ring[:, r, :], h2[:, t, :], 1.0, 0.0, ALU.mult,
                                                   ALU.add, dots_now[:, s % BODY:s % BODY + 1]).then_inc(rows_used, 1)
                    if s % BODY == BODY - 1:
                        dve.wait_ge(rows_used, i * SUB + (RING + start + s + 1))
                        at0 = t * SLOTS + first * SUB + s + 1 - BODY
                        nc.vector.tensor_copy(dots[:, bass.ds(i * SUB + at0, BODY)],
                                              dots_now[:]).then_inc(dots_saved, 1)
                        dve.wait_ge(dots_saved, i * (SUB // BODY) + (dots_before + s // BODY + 1))

                with dve.Fori(0, count) as i:
                    rows_and_columns(b, 0, t, i, take, first)

            def weigh(b):
                dve.wait_ge(gelu_ready, b + 1)
                n = GATHERED[b]
                d = dots[:, 0:n * SLOTS]
                link(nc.vector.tensor_tensor(d, d, gate[:, b, 0:n].rearrange("p t n -> p (t n)"), ALU.mult))

            def add_rows(b, t):
                def take(i, s, r, start):
                    dve.wait_ge(rows_used, i * SUB + (RING + start + s))
                    nc.vector.scalar_tensor_tensor(
                        out=x1s[b][:, t, :], in0=ring[:, r, :],
                        scalar=dots[:, bass.ds(i * SUB + (t * SLOTS + s), 1)],
                        in1=x1s[b][:, t, :], op0=ALU.mult, op1=ALU.add).then_inc(rows_used, 1)

                with dve.Fori(0, SUBS) as i:
                    rows_and_columns(b, 1, t, i, take)

            def split_ids(t):
                ids = idx[:, 1, t * SLOTS:(t + 1) * SLOTS]
                for a, (op, imm) in enumerate(((ALU.logical_shift_right, 7), (ALU.bitwise_and, N_KEYS - 1))):
                    link(nc.vector.tensor_scalar(part_u, ids, imm, None, op))
                    link(nc.vector.tensor_copy(parts[:, t - GATHERED[1], a, :], part_u))
                dve.sem_inc(parts_ready, 1)

            def one_hots(block):
                if block == 0:
                    for t in range(GATHERED[1], TT):
                        moved(dve, 1, "chosen", t)
                with dve.Fori(0, BLOCK // OH_RING) as i:
                    for r in range(OH_RING):
                        n = i * OH_RING + (block * BLOCK + r)
                        col = bass.ds(n, 1)
                        if r % 4 == 0:
                            dve.wait_ge(block_filled[r // 4], i + (block * BLOCK // OH_RING + 1))
                        nc.vector.tensor_scalar(one_hot_i[:, r, :], iota[:], chosen[:, 0, col], None, ALU.is_equal)
                        nc.vector.tensor_scalar(one_hot_j[:, r, :], iota[:], chosen[:, 1, col], chosen[:, 2, col],
                                                ALU.is_equal, ALU.mult).then_inc(one_hot_ready, 1)

            def add_dense():
                dve.wait_ge(col_added, N_KEYS + 2)
                for t in range(GATHERED[1], TT):
                    for n in range(2):
                        x = x1s[1][:, t, n * 512:(n + 1) * 512]
                        step(nc.vector.tensor_tensor(x, x, dense_out[2 * (t - GATHERED[1]) + n][:], ALU.add))
                    sync()
                    dve.sem_inc(dense_added, 1)

            def finish(b, t):
                dve.wait_ge(g_loaded, 32)
                dve.wait_ge(std3_ready, b * TT + t + 1)
                link(nc.vector.reciprocal(stat[:, 2, t:t + 1], stat[:, 2, t:t + 1]))
                nc.vector.scalar_tensor_tensor(out=x1s[b][:, t, :], in0=x1s[b][:, t, :], scalar=stat[:, 2, t:t + 1],
                                               in1=g_row[:], op0=ALU.mult, op1=ALU.mult).then_inc(y_ready, 1)

            step(nc.vector.memset(eps[:], EPS))
            dve.sem_inc(rows_used, RING)
            norm1(0)
            rotate(0)
            pool_out(0)
            attention(0, 0, n_att)
            attn_out(0, 0, KD)
            out(0)
            norm2(0)
            for hp in range(HALVES):
                top_halves(0, hp)
            merge(0, 0)

            between_dots = [
                [lambda: merge(0, 1)], [lambda: merge(0, 2)], [lambda: merge(0, 3), lambda: norm1(1)],
                [lambda: rotate(1)], [lambda: pool_out(1)],
                *[[lambda i=i: attention(1, 8 * i, 8 * i + 8)] for i in range(4)],
                [lambda: attn_out(1, 0, KD), lambda: out(1)], [lambda: norm2(1)],
                *[[lambda i=i, h=h: top_halves(1, 4 * i + h) for h in range(4)] for i in range(4)],
                [lambda t=t: merge(1, t) for t in range(TT)],
            ]
            for n in range(TT * SUBS):
                dot_rows(0, n // SUBS, n % SUBS, 1)
                for piece in between_dots[n]:
                    piece()
            for t in range(GATHERED[1], TT):
                split_ids(t)
            for block in range(BLOCKS):
                one_hots(block)
            weigh(0)
            for t in range(TT):
                add_rows(0, t)
            for t in range(TT):
                finish(0, t)
            for t in range(GATHERED[1]):
                dot_rows(1, t, 0, SUBS)
            weigh(1)
            for t in range(GATHERED[1]):
                add_rows(1, t)
                finish(1, t)
            add_dense()
            for t in range(GATHERED[1], TT):
                finish(1, t)


def shape_constants(np):
    band = np.zeros((P, GROUPS, BAND_W), np.float32)
    s, t = np.arange(T)[:, None], np.arange(T)[None, :]
    for g, w in enumerate(WINDOWS):
        lo, hi = np.clip(t - w // 2, 0, T), np.clip(t + w - w // 2, 0, T)
        m = ((s >= lo) & (s < hi)) / (hi - lo).astype(np.float32) - (s == t)
        for kind, tile in enumerate((0, 1, TT - 1)):
            band[:, g, kind * P:(kind + 1) * P] = m[tile * P:(tile + 1) * P, tile * P:(tile + 1) * P]
        band[:, g, 3 * P:3 * P + EDGE] = m[0:P, P:P + EDGE]
        band[:, g, 3 * P + EDGE:] = m[P:2 * P, P - EDGE:P]
    quarter = HD // 4
    inv = np.float32(ROPE_THETA) ** (-np.arange(quarter, dtype=np.float32) / np.float32(quarter))
    rope = np.zeros((P, TT, 2, 2, 2, quarter), np.float32)
    tok = np.arange(T).reshape(TT, P).T
    for axis, pos in enumerate((tok // GRID_W, tok % GRID_W)):
        ang = pos.astype(np.float32)[:, :, None] * inv.astype(np.float32)
        rope[:, :, 0, axis] = np.cos(ang)[:, :, None]
        rope[:, :, 1, axis, 0] = -np.sin(ang)
        rope[:, :, 1, axis, 1] = np.sin(ang)
    iota = np.broadcast_to(np.arange(P, dtype=np.float32), (P, P))
    return {"ident_c": np.eye(P, dtype=np.float32), "band_c": band,
            "rope_c": rope.reshape(P, TT, 2, HD), "iota_c": np.ascontiguousarray(iota)}


def kernel(**inputs):
    import numpy as np
    import concourse.bacc as bacc
    from concourse.bass_utils import run_bass_kernel_spmd

    a = {k: np.asarray(v) for k, v in inputs.items()}
    columns = lambda v, n: np.ascontiguousarray(v.reshape(n, P).T)
    arrays = {
        "x_prompt": a["x_prompt"], "x_sample": a["x_sample"], "w_in": a["w_in"][0], "pool_w": a["pool_w"][0],
        "w_pool_out": a["w_pool_out"][0], "w_attn_out": a["w_attn_out"][0], "w_out": a["w_out"][0],
        "w_query": a["w_query"][0],
        "keysT": a["sub_keys"][0].reshape(HALVES * N_KEYS, P).T,
        "expert_u": a["expert_u"][0], "expert_v": a["expert_v"][0],
        "expert_uT": a["expert_u"][0].reshape(N_KEYS, N_KEYS, KD, P).transpose(3, 1, 2, 0).reshape(P, N_KEYS, D),
        "g_mix": columns(a["g_mix"][0], KD), "pool_scale": columns(a["pool_scale"][0], GROUPS),
        "q_norm": a["q_norm"][0], "k_norm": a["k_norm"][0], "g_ffn": a["g_ffn"][0], "g_final": a["g_final"],
        **shape_constants(np),
    }
    nc = bacc.Bacc("TRN2", target_bir_lowering=False, num_devices=1)
    given, args = {}, []
    for name, v in arrays.items():
        v = np.ascontiguousarray(v)
        given[f"in_{name}"] = v
        args.append(nc.dram_tensor(f"in_{name}", v.shape, mybir.dt.from_np(v.dtype), kind="ExternalInput").ap())
    for n in range(BATCHES):
        args.append(nc.dram_tensor(f"out_{n}", (1, T, D), F32, kind="ExternalOutput").ap())
    encoder_kernel(nc, *args)
    r = run_bass_kernel_spmd(nc, [given], core_ids=[0])
    return tuple(r.results[0][f"out_{n}"] for n in range(BATCHES))
```

```python
from contextlib import ExitStack

import concourse.bass as bass
from concourse import mybir

ALU = mybir.AluOpType
ACT = mybir.ActivationFunctionType
AX = mybir.AxisListType
F32 = mybir.dt.float32
U32 = mybir.dt.uint32

P = 128
BATCHES = 2
T = 512
D = 1024
TT = T // P
KD = D // P
WINDOWS = (2, 4, 8, 16)
GROUPS = len(WINDOWS)
HEADS, KV_HEADS, HD = 8, 2, 64
PAIRS = HEADS // KV_HEADS
POOL_W, Q_W, KV_W = GROUPS * P, HEADS * HD, KV_HEADS * HD
QKV_W = Q_W + 2 * KV_W
QK_HEADS = HEADS + KV_HEADS
GRID_W = 64
ROPE_THETA = 10000.0
PEER_HEADS, N_KEYS, TOPK = 8, 128, 16
HALVES = 2 * PEER_HEADS
EPS = 1e-6
CHUNK = 256
LOWEST = -3.0e38

CAND_RUNS = []
CAND = 0
for _a in range(TOPK):
    _n = TOPK // (_a + 1)
    if CAND_RUNS and CAND_RUNS[-1][2] == _n:
        CAND_RUNS[-1][1] += 1
    else:
        CAND_RUNS.append([_a, 1, _n, CAND])
    CAND += _n

EDGE = 8
BAND_W = 3 * P + 2 * EDGE

BANKS = 6
WSLOTS = 4
RING = 8
BODY = 2 * RING
SUB = 2 * BODY
SLOTS = PEER_HEADS * TOPK
SUBS = SLOTS // SUB
GROUP_OF = ((0, (0,)), (0, (1, 2, 3)), (1, (0, 1, 2, 3)))
FIRST_GROUP, LAST_GROUP = (0, 2), (1, 2)
TILES_BEFORE = [sum(len(tiles) for _, tiles in GROUP_OF[:g]) for g in range(len(GROUP_OF) + 1)]
GATHERED = (TT, 1)
DENSE = TT - GATHERED[1]
DENSE_T = DENSE * P
PHASE_START = {(0, 0): 0, (0, 1): GATHERED[0] * SLOTS, (1, 0): 2 * GATHERED[0] * SLOTS,
               (1, 1): (2 * GATHERED[0] + GATHERED[1]) * SLOTS}
BLOCK = 32
BLOCKS = DENSE_T // BLOCK
OH_RING = 8
LONG = 2 * SUB
LONGS = SLOTS // LONG
UNIT_COLS = 4
PLACES = 4
UNITS_BESIDE = {(0, 1): 3, (1, 0): 3, (1, 1): 4}
SUMMED = 1
SUMMED_AFTER = RING
SUMMED_BEFORE = SLOTS - DENSE_T // OH_RING - SUMMED_AFTER
TURNS = {(0, 1): (GATHERED[0] - SUMMED) * LONGS, (1, 0): GATHERED[1] * LONGS, (1, 1): GATHERED[1] * LONGS}
UNITS_START, PLACE_LOADS = {}, {}
_units, _loads = 0, [0] * PLACES
for _key, _n in UNITS_BESIDE.items():
    UNITS_START[_key], PLACE_LOADS[_key] = _units, list(_loads)
    _units += TURNS[_key] * _n
    _loads = [_loads[_u] + (TURNS[_key] if _u < _n else 0) for _u in range(PLACES)]
assert _units == N_KEYS // UNIT_COLS

def attention_steps(g):
    return [(t, j, half) for t in GROUP_OF[g][1] for j in range(PAIRS) for half in range(KV_HEADS)]


STEPS_BEFORE = [HEADS * n for n in TILES_BEFORE]


def tile_pairs(g):
    tiles = GROUP_OF[g][1]
    return [tuple(t for t in (2 * tp, 2 * tp + 1) if t in tiles) for tp in sorted({t // 2 for t in tiles})]


BOTH = [(2 * tp, 2 * tp + 1) for tp in range(TT // 2)]


def jobs_of(g):
    b = GROUP_OF[g][0]
    heads = [((g, "q", c, tp), (g, "q", c)) for c in range(2) for tp in range(2)]
    heads += [((g, "kv", tp), (g, "kv")) for tp in range(2)]
    pool = [((g, "p", c, tp), (g, "p", c)) for c in range(2) for tp in range(2)]
    pool += [((g, name, pg), None) for name in ("pooled", "mixed") for pg in range(GROUPS)]
    gates = [((g, "gate_pool", d), (g, "gate_pool", d // 2)) for d in range(KD)]
    if g == FIRST_GROUP[b]:
        for k in range(KD):
            yield (g, "hT", k), None
    if g == FIRST_GROUP[0]:
        yield from heads + pool + gates
    elif g == FIRST_GROUP[1]:
        yield from gates + pool + heads
    else:
        yield from gates
    for d in range(KD):
        yield (g, "pool_out", d), (g, "pool_out", d // 4)
    if g == FIRST_GROUP[b]:
        for gg in range(g, LAST_GROUP[b] + 1):
            for j in range(PAIRS):
                yield (gg, "qT", j), None
        yield (g, "kT"), None
    n = len(attention_steps(g))
    yield (g, "s", 0), None
    yield (g, "s", 1), None
    for i in range(n):
        if i + 2 < n:
            yield (g, "s", i + 2), None
        yield (g, "probsT", i), None
    for c in range(KD // 2):
        for d in (2 * c, 2 * c + 1):
            yield (g, "gate_attn", d), (g, "gate_attn", c)
        for d in (2 * c, 2 * c + 1):
            yield (g, "attn_out", d), (g, "attn_out", d // 4)
    for c in range(D // CHUNK):
        for tp in tile_pairs(g):
            yield (g, "out", c, tp), (g, "out", c)
    for k in range(KD):
        yield (g, "h2T", k), None
    for c in range(HALVES // 2):
        for hp in (2 * c, 2 * c + 1):
            yield (g, "query", hp), (g, "query", c)
        for hp in (2 * c, 2 * c + 1):
            yield (g, "keys", hp), (g, "query", c)
    if g == LAST_GROUP[1]:
        yield (g, "sums", 0), None
        yield (g, "sums", 1), None
        for t in range(GATHERED[b], TT):
            yield (g, "chosen", t), None


JOB, CHUNKS, LAST_JOB = {}, [], {}
for _g in range(len(GROUP_OF)):
    for _job, _chunk in jobs_of(_g):
        JOB[_job] = len(JOB)
        if _chunk is not None:
            if _chunk not in LAST_JOB:
                CHUNKS.append(_chunk)
            LAST_JOB[_chunk] = _job


def chunk_order(g):
    return [c for c in CHUNKS if c[0] == g]


def token_cols(g):
    tiles = GROUP_OF[g][1]
    return slice(tiles[0] * P, (tiles[-1] + 1) * P)


def encoder_kernel(nc, x_prompt, x_sample, w_in, pool_w, w_pool_out, w_attn_out, w_out, w_query,
                   keysT, expert_u, expert_v, expert_uT, g_mix, pool_scale, q_norm, k_norm, g_ffn, g_final,
                   ident_c, band_c, rope_c, iota_c, y_prompt, y_sample):
    xs, ys = (x_prompt, x_sample), (y_prompt, y_sample)
    ctx = ExitStack()
    with ctx:
        def sb(name, shape, dt=F32):
            return ctx.enter_context(nc.sbuf_tensor(name, shape, dt))

        def sem(name):
            return ctx.enter_context(nc.semaphore(name))

        def sems(name, n):
            return [sem(f"{name}{i}") for i in range(n)]

        banks = [ctx.enter_context(nc.psum_tensor(f"bank{i}", [P, 512], F32)) for i in range(BANKS)]
        o_banks = [ctx.enter_context(nc.psum_tensor(f"o_bank{i}", [P, PAIRS, P], F32)) for i in range(2)]

        wslot = sb("wslot", [P, WSLOTS, KD * CHUNK])
        keys_sb = sb("keys_sb", [P, WSLOTS, 2 * N_KEYS])
        region_a = sb("region_a", [P, TT * D])
        region_b = sb("region_b", [P, TT * D])
        region_c = sb("region_c", [P, TT * D])
        h2 = sb("h2", [P, TT, D])
        ring = sb("ring", [P, RING, D])
        region_p = sb("region_p", [P, TT * POOL_W + GROUPS * T])
        region_q = sb("region_q", [P, TT * QKV_W + 2 * QK_HEADS * HD])
        region_s = sb("region_s", [P, 6 * T])
        gate_attn = sb("gate_attn", [P, 2, T])
        ident = sb("ident", [P, P])
        band = sb("band", [P, GROUPS, BAND_W])
        rope = sb("rope", [P, TT, 2, HD])
        iota = sb("iota", [P, P])
        pool_w_sb = sb("pool_w_sb", [P, GROUPS, P])
        g_mix_sb = sb("g_mix_sb", [P, KD])
        pool_scale_sb = sb("pool_scale_sb", [P, GROUPS])
        qk_norm_sb = sb("qk_norm_sb", [P, 2, HD])
        g_row = sb("g_row", [P, D])
        idx = sb("idx", [P, BATCHES, TT * SLOTS], U32)
        idx_now = sb("idx_now", [P, 2, RING], U32)
        gate = sb("gate", [P, BATCHES, TT, SLOTS])
        dots = sb("dots", [P, TT * SLOTS])
        gate_sum = sb("gate_sum", [P, TT * PEER_HEADS])
        dots_now = sb("dots_now", [P, BODY])
        stat = sb("stat", [P, 3, TT])
        head_stat = sb("head_stat", [P, TT, QK_HEADS])
        neg_max = sb("neg_max", [P, 2])
        prob_sum = sb("prob_sum", [P, 2])
        eps = sb("eps", [P, 1])

        xa = region_b[:, :].rearrange("p (t d) -> p t d", t=TT)
        hT = region_a[:, :].rearrange("p (k t) -> p k t", k=KD)
        gate_pool = region_b[:, :].rearrange("p (k t) -> p k t", k=KD)
        merged = gate_pool
        h2T = gate_pool
        x1s = [r[:, :].rearrange("p (t d) -> p t d", t=TT) for r in (region_c, region_a)]
        region_p0, region_p1 = region_p[:, 0:TT * POOL_W], region_p[:, TT * POOL_W:]
        pool_in = region_p0.rearrange("p (t c) -> p t c", t=TT)
        attnT = region_p0.rearrange("p (j t) -> p j t", j=PAIRS)
        pooledT = region_p1.rearrange("p (g t) -> p g t", g=GROUPS)
        late = region_c[:, D:]
        sizes = [PAIRS * P * len(tiles) for _, tiles in GROUP_OF]
        qTs = [region_p1[:, 0:sizes[0]].rearrange("p (j t) -> p j t", j=PAIRS),
               late[:, 0:sizes[1]].rearrange("p (j t) -> p j t", j=PAIRS),
               region_p1.rearrange("p (j t) -> p j t", j=PAIRS)]
        qkv = region_q[:, 0:TT * QKV_W].rearrange("p (t n) -> p t n", t=TT)
        vs = [late[:, sizes[1] + T:sizes[1] + T + TT * KV_W].rearrange("p (t n) -> p t n", t=TT),
              qkv[:, :, Q_W + KV_W:]]
        rope1 = region_q[:, TT * QKV_W:TT * QKV_W + QK_HEADS * HD]
        rope2 = region_q[:, TT * QKV_W + QK_HEADS * HD:]
        norm1_junk = gate_attn[:, :, :].rearrange("p a t -> p (a t)")
        last_junk = region_q[:, D:2 * D]
        norm2_junk = region_q[:, 0:D]
        h2_to_turn = [h2, region_q[:, 0:TT * D].rearrange("p (t d) -> p t d", t=TT)]
        mixedTs = [h2[:, 2:4, :].rearrange("p a d -> p (a d)").rearrange("p (g t) -> p g t", g=GROUPS),
                   region_s[:, 0:GROUPS * T].rearrange("p (g t) -> p g t", g=GROUPS)]
        kTs = [late[:, sizes[1]:sizes[1] + T], region_s[:, 0:T]]
        probs = region_s[:, T:3 * T].rearrange("p (a s) -> p a s", a=2)
        probsT = region_s[:, 3 * T:5 * T].rearrange("p (a s) -> p a s", a=2)
        peer_q = region_s[:, 0:2 * T].rearrange("p (a t) -> p a t", a=2)
        score = region_s[:, 2 * T:6 * T].rearrange("p (a t n) -> p a t n", a=4, t=TT)
        at = [0]

        def scratch(n):
            at[0] += n
            return region_q[:, at[0] - n:at[0]]

        best = scratch(TT * HALVES * TOPK).rearrange("p (t a k) -> p t a k", t=TT, a=HALVES)
        best_at = scratch(TT * HALVES * TOPK // 2).bitcast(mybir.dt.uint16).rearrange(
            "p (t a k) -> p t a k", t=TT, a=HALVES)
        sel_f = scratch(HALVES * TOPK).rearrange("p (a k) -> p a k", a=HALVES)
        cand = scratch(PEER_HEADS * CAND).rearrange("p (h n) -> p h n", h=PEER_HEADS)
        cand_id = scratch(PEER_HEADS * CAND).rearrange("p (h n) -> p h n", h=PEER_HEADS)
        match = [scratch(TOPK * CAND) for _ in range(2)]
        chosen = region_s[:, 0:3 * DENSE_T].rearrange("p (a t) -> p a t", a=3)
        parts = region_s[:, 3 * DENSE_T:5 * DENSE_T].rearrange("p (t a n) -> p t a n", t=DENSE, a=2)
        part_u = region_s[:, 5 * DENSE_T:5 * DENSE_T + SLOTS].bitcast(U32)
        one_hot_i = keys_sb[:, :, :].rearrange("p a (b n) -> p (a b) n", n=P)
        one_hot_j = gate_attn[:, :, :].rearrange("p a (b n) -> p (a b) n", n=P)
        blocks = [region_q[:, 0:N_KEYS * BLOCK], region_p[:, 0:N_KEYS * BLOCK]]
        weight_dram = nc.dram_tensor("expert_weights", (P, BLOCKS, N_KEYS, BLOCK), F32, kind="Internal").ap()
        u_cols = [wslot[:, n, 0:D].rearrange("p (k i) -> p k i", k=KD) for n in range(2)]
        v_cols = [wslot[:, 2 + n, 0:D] for n in range(2)]
        UNIT = UNIT_COLS * DENSE_T
        weights_in = [region_p[:, 0:UNIT], region_p[:, UNIT:2 * UNIT], region_s[:, 0:UNIT],
                      region_s[:, UNIT:2 * UNIT]]
        diag = region_s[:, 6 * T - RING * P:].rearrange("p (a n) -> p a n", n=P)
        hidden = [region_q[:, n * DENSE_T:(n + 1) * DENSE_T] for n in range(2)]
        dense_out = banks
        dense_in = [o[:, :, :].rearrange("p a b -> p (a b)") for o in o_banks]

        bank_filled, bank_freed = sems("bank_filled", BANKS), sems("bank_freed", BANKS)
        o_filled, o_freed = sems("o_filled", 2), sems("o_freed", 2)
        w_loaded = sems("w_loaded", WSLOTS)
        keys_loaded = sems("keys_loaded", WSLOTS)
        x_loaded = sems("x_loaded", TT)
        res_loaded = sem("res_loaded")
        first_loaded, consts_loaded = sem("first_loaded"), sem("consts_loaded")
        g_loaded = sem("g_loaded")
        act_step, dve_step = sem("act_step"), sem("dve_step")
        std_ready = sem("std_ready")
        xr_ready = sem("xr_ready")
        head_sq_ready, head_std_ready, roped = sem("head_sq_ready"), sem("head_std_ready"), sem("roped")
        pool_merged = sem("pool_merged")
        max_ready, exp_ready, probs_ready = sem("max_ready"), sem("exp_ready"), sem("probs_ready")
        merged_ready, x1_ready = sem("merged_ready"), sem("x1_ready")
        std2_ready, h2_ready = sem("std2_ready"), sem("h2_ready")
        halves_done = sem("halves_done")
        top_ready, top_exp = sem("top_ready"), sem("top_exp")
        idx_ready = sem("idx_ready")
        row_landed = sems("row_landed", RING)
        rows_used = sem("rows_used")
        idx_staged, slot_ok = sem("idx_staged"), sem("slot_ok")
        dots_saved, gelu_ready = sem("dots_saved"), sem("gelu_ready")
        weighed, diag_ready, sums_added = sem("weighed"), sem("diag_ready"), sem("sums_added")
        parts_ready, one_hot_ready = sem("parts_ready"), sem("one_hot_ready")
        block_filled, block_freed = sems("block_filled", 2), sems("block_freed", 2)
        block_moved, block_stored = sem("block_moved"), sems("block_stored", 2)
        u_loaded, v_loaded, weights_loaded = sems("u_loaded", 2), sems("v_loaded", 2), sems("weights_loaded", PLACES)
        col_filled, col_moved = sem("col_filled"), sem("col_moved")
        hidden_ready, col_added = sem("hidden_ready"), sem("col_added")
        dense_added = sem("dense_added")
        std3_ready, y_ready, y_stored = sem("std3_ready"), sem("y_ready"), sem("y_stored")

        def filled(eng, *job):
            n = JOB[job]
            eng.wait_ge(bank_filled[n % BANKS], n // BANKS + 1)
            return banks[n % BANKS]

        def moved(eng, *job):
            n = JOB[job]
            eng.wait_ge(bank_freed[n % BANKS], n // BANKS + 1)

        def frees(*job):
            return bank_freed[JOB[job] % BANKS]

        block = ctx.enter_context(nc.Block())

        @block.sync
        def _(sp):
            def load_x(b):
                if b:
                    filled(sp, LAST_GROUP[b - 1], "query", HALVES - 1)
                for t in range(TT):
                    sp.dma_start(xa[:, t, :], xs[b][0, t * P:(t + 1) * P, :]).then_inc(x_loaded[t], 16)

            def load_residual(g):
                b, tiles = GROUP_OF[g]
                if g:
                    filled(sp, g, "gate_attn", KD - 1)
                sp.dma_start(x1s[b][:, tiles[0]:tiles[-1] + 1, :],
                             xs[b][0].rearrange("(t p) d -> p t d", p=P)[:, tiles[0]:tiles[-1] + 1, :]).then_inc(
                                 res_loaded, 16)

            load_x(0)
            sp.dma_start(ident[:], ident_c).then_inc(first_loaded, 16)
            sp.dma_start(g_mix_sb[:], g_mix).then_inc(first_loaded, 16)

            w_in_cols = {"p": 0, "q": POOL_W, "kv": POOL_W + Q_W, "gate_pool": POOL_W + QKV_W,
                         "gate_attn": POOL_W + QKV_W + D}
            for g in range(len(GROUP_OF)):
                if g == FIRST_GROUP[1]:
                    load_x(1)
                for n, chunk in enumerate(chunk_order(g)):
                    m = CHUNKS.index(chunk)
                    if m >= WSLOTS:
                        filled(sp, *LAST_JOB[CHUNKS[m - WSLOTS]])
                    name, c = chunk[1], (chunk[2] if len(chunk) > 2 else 0)
                    dst = wslot[:, m % WSLOTS, :]
                    if name in w_in_cols:
                        at0 = w_in_cols[name] + c * CHUNK
                        src = w_in[:, at0:at0 + CHUNK].rearrange("(k p) n -> p k n", p=P)
                        dst = dst.rearrange("p (k n) -> p k n", k=KD)
                    elif name == "pool_out":
                        src = w_pool_out[:, c * 512:(c + 1) * 512].rearrange("(g p) n -> p g n", p=P)
                        dst = dst.rearrange("p (g n) -> p g n", g=GROUPS)
                    elif name == "attn_out":
                        dst = dst.rearrange("p (j n) -> p j n", j=PAIRS)
                        for half in range(KV_HEADS):
                            src = w_attn_out[half * PAIRS * HD:(half + 1) * PAIRS * HD,
                                             c * 512:(c + 1) * 512].rearrange("(j p) n -> p j n", p=HD)
                            sp.dma_start(dst[half * HD:(half + 1) * HD], src).then_inc(
                                w_loaded[m % WSLOTS], 16)
                        continue
                    else:
                        w = w_out if name == "out" else w_query
                        src = w[:, c * CHUNK:(c + 1) * CHUNK].rearrange("(k p) n -> p k n", p=P)
                        dst = dst.rearrange("p (k n) -> p k n", k=KD)
                    sp.dma_start(dst, src).then_inc(w_loaded[m % WSLOTS], 16)
                    if name == "query":
                        sp.dma_start(keys_sb[:, m % WSLOTS, :],
                                     keysT[:, c * 2 * N_KEYS:(c + 1) * 2 * N_KEYS]).then_inc(
                                         keys_loaded[m % WSLOTS], 16)
                    if g == 0 and n == 3:
                        sp.dma_start(rope[:], rope_c).then_inc(consts_loaded, 16)
                        sp.dma_start(qk_norm_sb[:, 0, :], q_norm.partition_broadcast(P)).then_inc(consts_loaded, 16)
                        sp.dma_start(qk_norm_sb[:, 1, :], k_norm.partition_broadcast(P)).then_inc(consts_loaded, 16)
                        sp.dma_start(band[:], band_c).then_inc(consts_loaded, 16)
                        sp.dma_start(pool_w_sb[:], pool_w.rearrange("g c d -> c g d")).then_inc(consts_loaded, 16)
                        sp.dma_start(pool_scale_sb[:], pool_scale).then_inc(consts_loaded, 16)
                        sp.dma_start(iota[:], iota_c).then_inc(consts_loaded, 16)
                        sp.dma_start(g_row[:], g_ffn.partition_broadcast(P)).then_inc(g_loaded, 16)
                    if name == "out" and c == 1:
                        load_residual(g)
            sp.wait_ge(h2_ready, TILES_BEFORE[-1])
            sp.dma_start(g_row[:], g_final.partition_broadcast(P)).then_inc(g_loaded, 16)

            for n in range(BLOCKS):
                sp.wait_ge(block_moved, 8 * (n + 1))
                sp.dma_start(weight_dram[:, n, :, :].rearrange("i j t -> i (j t)"),
                             blocks[n % 2]).then_inc(block_stored[n % 2], 16)
            for n in range(2):
                sp.wait_ge(block_stored[n], 16 * BLOCKS // 2)

            def load_column(j, q, waits):
                if waits:
                    sp.wait_ge(col_filled, j - 1)
                sp.dma_start(u_cols[q].rearrange("p k i -> p (k i)").unsqueeze(1),
                             expert_uT[:, bass.ds(j, 1), :]).then_inc(u_loaded[q], 16)
                if waits:
                    sp.wait_ge(col_added, j + 1)
                sp.dma_start(v_cols[q].unsqueeze(1),
                             expert_v.rearrange("(i j) d -> i j d", j=N_KEYS)[:, bass.ds(j, 1), :]).then_inc(
                                 v_loaded[q], 16)

            def load_weights(j, u, waits):
                if waits is not None:
                    sp.wait_ge(hidden_ready, waits)
                sp.dma_start(weights_in[u].rearrange("p (b j t) -> p b j t", j=UNIT_COLS, t=BLOCK),
                             weight_dram[:, :, bass.ds(j, UNIT_COLS), :]).then_inc(weights_loaded[u], 16)

            def load_units(key, i, first=False):
                units = UNITS_BESIDE[key]
                for u in range(units):
                    j = i * (units * UNIT_COLS) + (UNITS_START[key] + u) * UNIT_COLS
                    load_weights(j, u, None if first else i * (units * UNIT_COLS)
                                 + (UNITS_START[key] + u - units + 1) * UNIT_COLS)
                    for c in range(UNIT_COLS):
                        load_column(j + c, c % 2, not (first and u == 0 and c < 2))

            for key in UNITS_BESIDE:
                begin = 0
                if key == (0, 1):
                    load_units(key, 0, True)
                    begin = 1
                else:
                    sp.wait_ge(hidden_ready, UNITS_START[key] * UNIT_COLS)
                with sp.Fori(begin, TURNS[key]) as i:
                    load_units(key, i)

        FIRST_ALL, CONSTS_ALL = 2 * 16, 7 * 16

        def chunk_landed(eng, chunk):
            m = CHUNKS.index(chunk)
            count = 0
            for n in range(m % WSLOTS, m + 1, WSLOTS):
                count += 2 if CHUNKS[n][1] == "attn_out" else 1
            eng.wait_ge(w_loaded[m % WSLOTS], 16 * count)
            return m % WSLOTS

        @block.tensor
        def _(pe):
            def fill(*job):
                n = JOB[job]
                if n >= BANKS:
                    pe.wait_ge(bank_freed[n % BANKS], n // BANKS)
                return banks[n % BANKS]

            def done(ins, *job):
                ins.then_inc(bank_filled[JOB[job] % BANKS], 1)

            def turned(job, tiles, src):
                bank = fill(*job)
                for n, t in enumerate(tiles):
                    ins = nc.tensor.transpose(bank[:, n * P:(n + 1) * P], src(t), ident[:])
                done(ins, *job)

            def token_major(job, chunk, lhs, tp):
                slot = chunk_landed(pe, chunk)
                w = wslot[:, slot, :].rearrange("p (k n) -> p k n", k=KD)
                bank = fill(*job)
                for tt, t in enumerate(tp):
                    for k in range(KD):
                        ins = nc.tensor.matmul(bank[:, tt * CHUNK:(tt + 1) * CHUNK],
                                               lhs[:, k, t * P:(t + 1) * P], w[:, k, :],
                                               start=(k == 0), stop=(k == KD - 1))
                done(ins, *job)

            def feature_major(job, chunk, rhs, col, steps):
                slot = chunk_landed(pe, chunk)
                w = wslot[:, slot, :].rearrange("p (k n) -> p k n", k=steps)
                cols = token_cols(job[0])
                bank = fill(*job)
                for k in range(steps):
                    ins = nc.tensor.matmul(bank[:, 0:cols.stop - cols.start], w[:, k, col:col + P],
                                           rhs[:, k, cols], start=(k == 0), stop=(k == steps - 1))
                done(ins, *job)

            def turn_h(g):
                b = GROUP_OF[g][0]
                if b == 0:
                    pe.wait_ge(first_loaded, FIRST_ALL)
                pe.wait_ge(xr_ready, TT * (b + 1))
                for k in range(KD):
                    turned((g, "hT", k), range(TT), lambda t: xa[:, t, k * P:(k + 1) * P])
                for k in range(KD):
                    moved(pe, g, "hT", k)

            def project_heads(g):
                for c in range(2):
                    for tp in range(2):
                        token_major((g, "q", c, tp), (g, "q", c), hT, BOTH[tp])
                for tp in range(2):
                    token_major((g, "kv", tp), (g, "kv"), hT, BOTH[tp])

            def project_pool(g):
                for c in range(2):
                    for tp in range(2):
                        token_major((g, "p", c, tp), (g, "p", c), hT, BOTH[tp])
                if g == 0:
                    pe.wait_ge(consts_loaded, CONSTS_ALL)
                for pg in range(GROUPS):
                    for tp in range(2):
                        moved(pe, g, "p", pg // 2, tp)
                    bank = fill(g, "pooled", pg)
                    cols = slice(pg * P, (pg + 1) * P)
                    for t in range(TT):
                        kind = 0 if t == 0 else (2 if t == TT - 1 else 1)
                        ins = nc.tensor.matmul(bank[:, t * P:(t + 1) * P], pool_in[:, t, cols],
                                               band[:, pg, kind * P:(kind + 1) * P], start=True,
                                               stop=False, skip_group_check=True)
                        if t > 0:
                            ins = nc.tensor.matmul(bank[:, t * P:t * P + EDGE], pool_in[:, t - 1, cols],
                                                   band[:, pg, 3 * P:3 * P + EDGE], start=False,
                                                   stop=(t == TT - 1), skip_group_check=True)
                        if t < TT - 1:
                            ins = nc.tensor.matmul(bank[:, (t + 1) * P - EDGE:(t + 1) * P],
                                                   pool_in[:, t + 1, cols],
                                                   band[:, pg, 3 * P + EDGE:], start=False,
                                                   stop=True, skip_group_check=True)
                    done(ins, g, "pooled", pg)
                for pg in range(GROUPS):
                    moved(pe, g, "pooled", pg)
                    bank = fill(g, "mixed", pg)
                    ins = nc.tensor.matmul(bank[:], pool_w_sb[:, pg, :], pooledT[:, pg, :], start=True, stop=True)
                    done(ins, g, "mixed", pg)

            def attention(g):
                b = GROUP_OF[g][0]
                steps = attention_steps(g)
                t0 = GROUP_OF[g][1][0]

                def scores(i):
                    t, j, half = steps[i]
                    if i == 0:
                        moved(pe, FIRST_GROUP[b], "kT")
                        for jj in range(PAIRS):
                            moved(pe, g, "qT", jj)
                    bank = fill(g, "s", i)
                    rows = slice(half * HD, (half + 1) * HD)
                    ins = nc.tensor.matmul(bank[:], qTs[g][rows, j, (t - t0) * P:(t - t0 + 1) * P],
                                           kTs[b][rows, :], start=True, stop=True)
                    done(ins, g, "s", i)

                def values(i):
                    t, j, half = steps[i]
                    if j == 0 and half == 0 and b * TT + t >= 2:
                        pe.wait_ge(o_freed[t % 2], (b * TT + t) // 2)
                    moved(pe, g, "probsT", i)
                    for s in range(TT):
                        ins = nc.tensor.matmul(o_banks[t % 2][half * HD:(half + 1) * HD, j, :],
                                               vs[b][:, s, half * HD:(half + 1) * HD],
                                               probsT[:, i % 2, s * P:(s + 1) * P],
                                               start=(s == 0), stop=(s == TT - 1))
                    if j == PAIRS - 1 and half == 1:
                        ins.then_inc(o_filled[t % 2], 1)

                scores(0)
                scores(1)
                for i in range(len(steps)):
                    if i + 2 < len(steps):
                        scores(i + 2)
                    pe.wait_ge(probs_ready, STEPS_BEFORE[g] + i + 1)
                    turned((g, "probsT", i), range(TT), lambda s: probs[:, i % 2, s * P:(s + 1) * P])
                    if i:
                        values(i - 1)
                values(len(steps) - 1)

            for g, (b, tiles) in enumerate(GROUP_OF):
                if g == FIRST_GROUP[b]:
                    turn_h(g)
                if g == FIRST_GROUP[0]:
                    project_heads(g)
                    project_pool(g)
                for d in range(KD):
                    feature_major((g, "gate_pool", d), (g, "gate_pool", d // 2), hT, d % 2 * P, KD)
                if g == FIRST_GROUP[1]:
                    project_pool(g)
                    project_heads(g)
                if g == FIRST_GROUP[b]:
                    for pg in range(GROUPS):
                        moved(pe, g, "mixed", pg)
                for d in range(KD):
                    feature_major((g, "pool_out", d), (g, "pool_out", d // 4), mixedTs[b], d % 4 * P, GROUPS)
                if g == FIRST_GROUP[b]:
                    pe.wait_ge(roped, TT * (b + 1))
                    for gg in range(g, LAST_GROUP[b] + 1):
                        for j in range(PAIRS):
                            turned((gg, "qT", j), GROUP_OF[gg][1], lambda t: qkv[:, t, j * P:(j + 1) * P])
                    turned((g, "kT"), range(TT), lambda t: qkv[:, t, Q_W:Q_W + KV_W])
                attention(g)
                for c in range(KD // 2):
                    for d in (2 * c, 2 * c + 1):
                        feature_major((g, "gate_attn", d), (g, "gate_attn", c), hT, d % 2 * P, KD)
                    if c == 0:
                        for t in tiles[-2:]:
                            pe.wait_ge(o_freed[t % 2], (b * TT + t) // 2 + 1)
                    for d in (2 * c, 2 * c + 1):
                        feature_major((g, "attn_out", d), (g, "attn_out", d // 4), attnT, d % 4 * P, PAIRS)
                pe.wait_ge(merged_ready, KD * (g + 1))
                for c in range(D // CHUNK):
                    for tp in tile_pairs(g):
                        token_major((g, "out", c, tp), (g, "out", c), merged, tp)
                pe.wait_ge(h2_ready, TILES_BEFORE[g + 1])
                for k in range(KD):
                    turned((g, "h2T", k), tiles, lambda t: h2_to_turn[b][:, t, k * P:(k + 1) * P])
                for k in range(KD):
                    moved(pe, g, "h2T", k)
                for c in range(HALVES // 2):
                    for hp in (2 * c, 2 * c + 1):
                        feature_major((g, "query", hp), (g, "query", c), h2T, hp % 2 * P, KD)
                    m = CHUNKS.index((g, "query", c))
                    pe.wait_ge(keys_loaded[m % WSLOTS],
                               16 * sum(CHUNKS[n][1] == "query" for n in range(m % WSLOTS, m + 1, WSLOTS)))
                    for hp in (2 * c, 2 * c + 1):
                        moved(pe, g, "query", hp)
                        bank = fill(g, "keys", hp)
                        for n in range(len(tiles)):
                            ins = nc.tensor.matmul(bank[:, n * P:(n + 1) * P],
                                                   peer_q[:, hp % 2, n * P:(n + 1) * P],
                                                   keys_sb[:, m % WSLOTS, hp % 2 * N_KEYS:(hp % 2 + 1) * N_KEYS],
                                                   start=True, stop=True)
                        done(ins, g, "keys", hp)

            b, g = 1, LAST_GROUP[1]
            for n in range(2):
                fill(g, "sums", n)

            def sum_half(i, r, n, start=False):
                if n == 0:
                    pe.wait_ge(row_landed[r], (i + (PHASE_START[0, 1] // RING + 1)) * 16)
                    pe.wait_ge(diag_ready, i * RING + (r + 1))
                ins = nc.tensor.matmul(banks[JOB[g, "sums", n] % BANKS][:], diag[:, r, :],
                                       ring[:, r, n * 512:(n + 1) * 512], start=start, stop=True,
                                       skip_group_check=True)
                if n == 1:
                    ins.then_inc(rows_used, 1)

            def sum_rows(i, r, start=False):
                for n in range(2):
                    sum_half(i, r, n, start)

            for r in range(RING):
                sum_rows(0, r, start=(r == 0))
            with pe.Fori(1, SUMMED_BEFORE // RING) as i:
                for r in range(RING):
                    sum_rows(i, r)
            for t in range(GATHERED[b], TT):
                pe.wait_ge(parts_ready, t - GATHERED[b] + 1)
                bank = fill(g, "chosen", t)
                for a, src in enumerate((parts[:, t - GATHERED[b], 0, :], parts[:, t - GATHERED[b], 1, :],
                                         gate[:, b, t, :])):
                    ins = nc.tensor.transpose(bank[:, a * P:(a + 1) * P], src, ident[:])
                done(ins, g, "chosen", t)
            for n in range(2):
                pe.sem_inc(block_filled[n], 1)
            pe.sem_inc(col_added, 2)
            with pe.Fori(0, DENSE_T // OH_RING // RING) as i:
                for v in range(RING):
                    for r in range(OH_RING):
                        pe.wait_ge(one_hot_ready, i * (RING * OH_RING) + (v * OH_RING + r + 1))
                        if r % 4 == 0:
                            pe.wait_ge(block_freed[r // 4], i * RING + (v + 1))
                        ins = nc.tensor.matmul(dense_in[r // 4][:, r % 4 * P:(r % 4 + 1) * P], one_hot_i[:, r, :],
                                               one_hot_j[:, r, :], start=True, stop=True)
                        if r % 4 == 3:
                            ins.then_inc(block_filled[r // 4], 1)
                            sum_half(i + SUMMED_BEFORE // RING, v, r // 4)
            with pe.Fori((SLOTS - SUMMED_AFTER) // RING, SLOTS // RING) as i:
                for r in range(RING):
                    sum_rows(i, r)

            def take_column(j, q, turn):
                pe.wait_ge(u_loaded[q], turn * 16)
                if isinstance(j, int) and j < 2:
                    for n in range(2):
                        pe.wait_ge(block_freed[n], DENSE_T // OH_RING + 1)
                else:
                    pe.wait_ge(col_moved, j - 1)
                for k in range(KD):
                    ins = nc.tensor.matmul(dense_in[q][:, 0:DENSE_T], u_cols[q][:, k, :],
                                           h2T[:, k, T - DENSE_T:T], start=(k == 0), stop=(k == KD - 1))
                ins.then_inc(col_filled, 1)

            def add_column(j, q, turn, start=False, stop=False):
                pe.wait_ge(v_loaded[q], turn * 16)
                pe.wait_ge(hidden_ready, j + 1)
                for t in range(DENSE):
                    for n in range(2):
                        ins = nc.tensor.matmul(dense_out[2 * t + n][:], hidden[q][:, t * P:(t + 1) * P],
                                               v_cols[q][:, n * 512:(n + 1) * 512], start=start, stop=stop,
                                               skip_group_check=True)
                ins.then_inc(col_added, 1)

            take_column(0, 0, 1)
            take_column(1, 1, 1)
            for t in range(GATHERED[b], TT):
                moved(pe, g, "chosen", t)
            for n in range(2):
                moved(pe, g, "sums", n)
            add_column(0, 0, 1, start=True)
            with pe.Fori(0, (N_KEYS - 2) // 2) as i:
                take_column(i * 2 + 2, 0, i + 2)
                add_column(i * 2 + 1, 1, i + 1)
                take_column(i * 2 + 3, 1, i + 2)
                add_column(i * 2 + 2, 0, i + 2)
            add_column(N_KEYS - 1, 1, N_KEYS // 2, stop=True)

        @block.scalar
        def _(act):
            n_act = [0]

            def link(ins):
                n_act[0] += 1
                ins.then_inc(act_step, 1)
                act.wait_ge(act_step, n_act[0])

            def move(dst, job, func=ACT.Identity, scale=1.0, view=None):
                bank = filled(act, *job)
                src = bank[:] if view is None else view(bank)
                nc.scalar.activation(dst, src, func, scale=scale).then_inc(frees(*job), 1)

            def norm1(b):
                if b:
                    act.wait_ge(merged_ready, KD * FIRST_GROUP[b])
                for t in range(TT):
                    act.wait_ge(x_loaded[t], 16 * (b + 1))
                    link(nc.scalar.activation(norm1_junk, xa[:, t, :], ACT.Square, accum_out=stat[:, 0, t:t + 1]))
                nc.scalar.activation(stat[:, 0, :], stat[:, 0, :], ACT.Sqrt, bias=eps[:],
                                     scale=1.0 / D).then_inc(std_ready, 1)

            def turned_h(b):
                g = FIRST_GROUP[b]
                if b == 0:
                    act.wait_ge(first_loaded, FIRST_ALL)
                for k in range(KD):
                    move(hT[:, k, :], (g, "hT", k), scale=g_mix_sb[:, k:k + 1])

            pair = lambda bank: bank[:].rearrange("p (t n) -> p t n", t=2)

            def projected_heads(b):
                g = FIRST_GROUP[b]
                if b:
                    act.wait_ge(top_ready, TT * b)
                for c in range(2):
                    for tp in range(2):
                        move(qkv[:, 2 * tp:2 * tp + 2, c * CHUNK:(c + 1) * CHUNK], (g, "q", c, tp), view=pair)
                for tp in range(2):
                    both = slice(2 * tp, 2 * tp + 2)
                    bank = pair(filled(act, g, "kv", tp))
                    nc.scalar.activation(qkv[:, both, Q_W:Q_W + KV_W], bank[:, :, 0:KV_W], ACT.Identity)
                    nc.scalar.activation(vs[b][:, both, :], bank[:, :, KV_W:], ACT.Identity).then_inc(
                        frees(g, "kv", tp), 1)

            def head_roots(b):
                act.wait_ge(head_sq_ready, b + 1)
                nc.scalar.activation(head_stat[:], head_stat[:], ACT.Sqrt, bias=eps[:],
                                     scale=1.0 / HD).then_inc(head_std_ready, 1)

            def projected_pool(b):
                g = FIRST_GROUP[b]
                for c in range(2):
                    for tp in range(2):
                        move(pool_in[:, 2 * tp:2 * tp + 2, c * CHUNK:(c + 1) * CHUNK], (g, "p", c, tp), view=pair)
                if b == 0:
                    head_roots(b)
                for pg in range(GROUPS):
                    move(pooledT[:, pg, :], (g, "pooled", pg))
                if b == 0:
                    act.wait_ge(consts_loaded, CONSTS_ALL)
                for pg in range(GROUPS):
                    move(mixedTs[b][:, pg, :], (g, "mixed", pg), scale=pool_scale_sb[:, pg:pg + 1])

            def some(g):
                return lambda bank: bank[:, 0:len(GROUP_OF[g][1]) * P]

            def pool_gates(g):
                for d in range(KD):
                    move(gate_pool[:, d, token_cols(g)], (g, "gate_pool", d), ACT.Sigmoid, view=some(g))

            def attention(g):
                b = GROUP_OF[g][0]
                n, before = len(attention_steps(g)), STEPS_BEFORE[g]
                if g == FIRST_GROUP[b]:
                    for gg in range(g, LAST_GROUP[b] + 1):
                        for j in range(PAIRS):
                            move(qTs[gg][:, j, :], (gg, "qT", j), scale=HD ** -0.5, view=some(gg))
                    move(kTs[b], (g, "kT"))

                def exp(i):
                    bank = filled(act, g, "s", i)
                    act.wait_ge(max_ready, before + i + 1)
                    if i >= 2:
                        filled(act, g, "probsT", i - 2)
                    nc.scalar.activation(probs[:, i % 2, :], bank[:], ACT.Exp, bias=neg_max[:, i % 2:i % 2 + 1],
                                         accum_out=prob_sum[:, i % 2:i % 2 + 1]).then_inc(exp_ready, 1)

                def outputs(t):
                    act.wait_ge(o_filled[t % 2], (b * TT + t) // 2 + 1)
                    nc.scalar.activation(attnT[:, :, t * P:(t + 1) * P], o_banks[t % 2][:],
                                         ACT.Identity).then_inc(o_freed[t % 2], 1)

                exp(0)
                for i in range(n):
                    if i + 1 < n:
                        exp(i + 1)
                    if g:
                        moved(act, g, "s", i)
                        nc.scalar.activation(probs[:, i % 2, :], probs[:, i % 2, :], ACT.Identity,
                                             scale=prob_sum[:, i % 2:i % 2 + 1]).then_inc(probs_ready, 1)
                    move(probsT[:, i % 2, :], (g, "probsT", i))
                    if i % HEADS == 0 and i:
                        outputs(GROUP_OF[g][1][i // HEADS - 1])
                outputs(GROUP_OF[g][1][-1])

            def gates(g):
                for d in range(KD):
                    if d >= 2:
                        act.wait_ge(merged_ready, g * KD + d - 1)
                    move(gate_attn[:, d % 2, token_cols(g)], (g, "gate_attn", d), ACT.Sigmoid, view=some(g))

            def norm2(g):
                b, tiles = GROUP_OF[g]
                act.wait_ge(x1_ready, g + 1)
                for t in tiles:
                    link(nc.scalar.activation(norm2_junk, x1s[b][:, t, :], ACT.Square, accum_out=stat[:, 1, t:t + 1]))
                st = stat[:, 1, tiles[0]:tiles[-1] + 1]
                nc.scalar.activation(st, st, ACT.Sqrt, bias=eps[:], scale=1.0 / D).then_inc(std2_ready, 1)

            def queries(g):
                tiles = GROUP_OF[g][1]
                for k in range(KD):
                    move(h2T[:, k, token_cols(g)], (g, "h2T", k), view=some(g))
                for c in range(HALVES // 2):
                    for hp in (2 * c, 2 * c + 1):
                        move(peer_q[:, hp % 2, 0:len(tiles) * P], (g, "query", hp), view=some(g))
                    for hp in (2 * c, 2 * c + 1):
                        if hp >= 4:
                            act.wait_ge(halves_done, g * HALVES + hp - 3)
                        move(score[:, hp % 4, 0:len(tiles), :], (g, "keys", hp),
                             view=lambda bank: some(g)(bank).rearrange("p (t n) -> p t n", n=N_KEYS))

            def gate_exp(b):
                act.wait_ge(top_ready, TT * (b + 1))
                g = gate[:, b]
                nc.scalar.activation(g, g, ACT.Exp).then_inc(top_exp, 1)

            def gelu(b):
                act.wait_ge(dots_saved, sum(GATHERED[:b + 1]) * SLOTS // BODY)
                d = dots[:, 0:GATHERED[b] * SLOTS]
                nc.scalar.activation(d, d, ACT.Gelu).then_inc(gelu_ready, 1)

            def diagonal(i, r):
                act.wait_ge(rows_used, i * RING + (PHASE_START[0, 1] + r + 1))
                nc.scalar.activation(diag[:, r, :], ident[:], ACT.Identity,
                                     scale=dots[:, bass.ds(i * RING + r, 1)]).then_inc(diag_ready, 1)

            def store_weights():
                for t in range(GATHERED[1], TT):
                    c = chosen[:, :, (t - GATHERED[1]) * P:(t - GATHERED[1] + 1) * P]
                    move(c, (LAST_GROUP[1], "chosen", t),
                         view=lambda bank: bank[:, 0:3 * P].rearrange("p (a t) -> p a t", a=3))
                for n in range(2):
                    act.sem_inc(block_freed[n], 1)

                def pair(i, stored):
                    turn = i * (2 * BLOCK // 8)
                    for n in range(2):
                        if stored is not None:
                            act.wait_ge(block_stored[n], stored)
                        dst = blocks[n].rearrange("p (j t) -> p t j", t=BLOCK)
                        for q in range(BLOCK // 4):
                            if q % 2 == 0:
                                diagonal(i + SUMMED_BEFORE // RING, n * BLOCK // 8 + q // 2)
                            act.wait_ge(block_filled[q % 2], turn + (n * BLOCK // 8 + q // 2 + 2))
                            nc.scalar.activation(dst[:, 4 * q:4 * q + 4, :],
                                                 dense_in[q % 2].rearrange("p (t j) -> p t j", t=4),
                                                 ACT.Identity).then_inc(block_freed[q % 2], 1)
                            act.wait_ge(block_freed[q % 2], turn + (n * BLOCK // 8 + q // 2 + 2))
                            act.sem_inc(block_moved, 1)

                pair(0, None)
                with act.Fori(1, BLOCKS // 2) as i:
                    pair(i, i * 16)
                with act.Fori((SLOTS - SUMMED_AFTER) // RING, SLOTS // RING) as i:
                    for r in range(RING):
                        diagonal(i, r)

            def hidden_columns(first, count):
                with act.Fori(0, count // 2) as i:
                    for q in range(2):
                        j = i * 2 + (first + q)
                        act.wait_ge(col_filled, j + 1)
                        act.wait_ge(col_added, j + 1)
                        nc.scalar.activation(hidden[q], dense_in[q][:, 0:DENSE_T], ACT.Gelu).then_inc(col_moved, 1)

            def finish(b, t):
                if b == 0 and t < SUMMED:
                    act.wait_ge(sums_added, 1)
                elif t < GATHERED[b]:
                    act.wait_ge(rows_used, RING + PHASE_START[b, 1] + (t + 1) * SLOTS)
                else:
                    act.wait_ge(dense_added, t - GATHERED[b] + 1)
                link(nc.scalar.activation(last_junk, x1s[b][:, t, :], ACT.Square, accum_out=stat[:, 2, t:t + 1]))
                nc.scalar.activation(stat[:, 2, t:t + 1], stat[:, 2, t:t + 1], ACT.Sqrt, bias=eps[:],
                                     scale=1.0 / D).then_inc(std3_ready, 1)
                act.wait_ge(y_ready, b * TT + t + 1)
                act.dma_start(ys[b][0, t * P:(t + 1) * P, :], x1s[b][:, t, :]).then_inc(y_stored, 16)

            def group(g):
                attention(g)
                gates(g)
                norm2(g)
                queries(g)

            act.wait_ge(dve_step, 1)
            norm1(0)
            turned_h(0)
            projected_heads(0)
            projected_pool(0)
            pool_gates(0)
            group(0)
            pool_gates(1)
            group(1)
            norm1(1)
            turned_h(1)
            pool_gates(2)
            projected_pool(1)
            projected_heads(1)
            head_roots(1)
            gate_exp(0)
            group(2)
            gelu(0)
            act.wait_ge(weighed, 1)
            with act.Fori(0, SUMMED_BEFORE // RING) as i:
                for r in range(RING):
                    diagonal(i, r)
            gate_exp(1)
            store_weights()
            for n in range(2):
                act.wait_ge(block_stored[n], 16 * BLOCKS // 2)
            START = {key: UNITS_START[key] * UNIT_COLS for key in UNITS_START}
            hidden_columns(0, START[1, 0])
            for t in range(TT):
                finish(0, t)
            hidden_columns(START[1, 0], START[1, 1] - START[1, 0])
            gelu(1)
            hidden_columns(START[1, 1], N_KEYS - START[1, 1])
            for t in range(TT):
                finish(1, t)
            act.wait_ge(y_stored, 16 * BATCHES * TT)

        @block.gpsimd
        def _(pool):
            for b in range(BATCHES):
                for phase, table in enumerate((expert_u, expert_v)):
                    base = PHASE_START[b, phase]
                    for t in range(GATHERED[b]):
                        pool.wait_ge(idx_ready, b * TT + t + 1)
                        with pool.Fori(0, SLOTS // BODY) as i:
                            for half in range(2):
                                n0 = i * BODY + base + t * SLOTS + half * RING
                                pool.wait_ge(rows_used, n0 + 1)
                                pool.sem_inc(slot_ok, 1)
                                nc.gpsimd.tensor_copy(
                                    idx_now[:, half, :],
                                    idx[:, b, bass.ds(i * BODY + t * SLOTS + half * RING, RING)]).then_inc(idx_staged, 1)
                                pool.wait_ge(idx_staged, (i * 2 + half + 1) + (base + t * SLOTS) // RING)
                                for r in range(RING):
                                    pool.wait_ge(rows_used, n0 + r + 1)
                                    pool.sem_inc(slot_ok, 1)
                                    nc.gpsimd.indirect_dma_start(
                                        ring[:, r, :], None, table,
                                        bass.IndirectOffsetOnAxis(ap=idx_now[:, half, r:r + 1], axis=0)).then_inc(row_landed[r], 16)

        @block.vector
        def _(dve):
            n_dve = [0]

            def step(ins):
                n_dve[0] += 1
                ins.then_inc(dve_step, 1)
                return n_dve[0]

            def after(n):
                dve.wait_ge(dve_step, n)

            def sync():
                dve.wait_ge(dve_step, n_dve[0])

            def link(ins):
                step(ins)
                sync()

            dotted = [0]

            def dot(count):
                for n in range(dotted[0], dotted[0] + count):
                    dve.wait_ge(row_landed[n % RING], 16 * (n // RING + 1))
                    row = ring[:, n % RING, :]
                    nc.vector.tensor_tensor_reduce(row, row, h2[:, n // SLOTS, :], 1.0, 0.0, ALU.mult, ALU.add,
                                                   dots[:, n:n + 1]).then_inc(rows_used, 1)
                    if n % BODY == BODY - 1:
                        dve.wait_ge(rows_used, RING + n + 1)
                        dve.sem_inc(dots_saved, 1)
                dotted[0] += count

            def dot_to(bodies):
                dot(-dotted[0] % BODY)
                while dotted[0] < bodies * BODY:
                    t, first = divmod(dotted[0], SLOTS)
                    count = min(bodies * BODY - dotted[0], SLOTS - first)
                    dot_rows(0, t, first, BODY, count // BODY)
                    dotted[0] += count

            def norm1(b):
                dve.wait_ge(std_ready, b + 1)
                link(nc.vector.reciprocal(stat[:, 0, :], stat[:, 0, :]))
                for t in range(TT):
                    nc.vector.tensor_scalar(xa[:, t, :], xa[:, t, :], stat[:, 0, t:t + 1], None,
                                            ALU.mult).then_inc(xr_ready, 1)

            def rotate(b, rows=0):
                if b == 0:
                    dve.wait_ge(consts_loaded, CONSTS_ALL)
                for t in range(TT):
                    if t % 2 == 0:
                        for c in range(2):
                            moved(dve, FIRST_GROUP[b], "q", c, t // 2)
                        moved(dve, FIRST_GROUP[b], "kv", t // 2)
                    dot(rows)
                    qk = qkv[:, t, 0:Q_W + KV_W]
                    link(nc.vector.tensor_tensor(rope1, qk, qk, ALU.mult))
                    link(nc.vector.tensor_reduce(head_stat[:, t, :], rope1.rearrange("p (h d) -> p h d", d=HD),
                                                 AX.X, ALU.add))
                dve.sem_inc(head_sq_ready, 1)
                dve.wait_ge(head_std_ready, b + 1)
                link(nc.vector.reciprocal(head_stat[:], head_stat[:]))
                for t in range(TT):
                    dot(rows)
                    heads = qkv[:, t, 0:Q_W + KV_W].rearrange("p (h d) -> p h d", d=HD)
                    r1, r2 = (r.rearrange("p (h d) -> p h d", d=HD) for r in (rope1, rope2))
                    link(nc.vector.tensor_tensor(r1, heads, head_stat[:, t, :].unsqueeze(2).to_broadcast(
                        [P, QK_HEADS, HD]), ALU.mult))
                    step(nc.vector.tensor_tensor(heads[:, 0:HEADS, :], r1[:, 0:HEADS, :],
                                                 qk_norm_sb[:, 0:1, :].to_broadcast([P, HEADS, HD]), ALU.mult))
                    link(nc.vector.tensor_tensor(heads[:, HEADS:, :], r1[:, HEADS:, :],
                                                 qk_norm_sb[:, 1:2, :].to_broadcast([P, KV_HEADS, HD]), ALU.mult))
                    step(nc.vector.tensor_tensor(r1, heads, rope[:, t, 0:1, :].to_broadcast([P, QK_HEADS, HD]),
                                                 ALU.mult))
                    for q in range(2):
                        src = heads.rearrange("p h (a q d) -> p h a q d", a=2, q=2)[:, :, :, 1 - q, :]
                        dst = r2.rearrange("p h (a q d) -> p h a q d", a=2, q=2)[:, :, :, q, :]
                        sin = rope[:, t, 1:2, :].rearrange("p o (a q d) -> p o a q d", a=2, q=2)[:, :, :, q, :]
                        step(nc.vector.tensor_tensor(dst, src, sin.to_broadcast([P, QK_HEADS, 2, HD // 4]), ALU.mult))
                    sync()
                    pairs = qkv[:, t, 0:Q_W].rearrange("p (j a d) -> p a j d", j=PAIRS, d=HD)
                    for half in range(KV_HEADS):
                        hs = slice(half * PAIRS, (half + 1) * PAIRS)
                        step(nc.vector.tensor_tensor(pairs[:, half], r1[:, hs, :], r2[:, hs, :], ALU.add))
                    link(nc.vector.tensor_tensor(heads[:, HEADS:, :], r1[:, HEADS:, :], r2[:, HEADS:, :], ALU.add))
                    dve.sem_inc(roped, 1)

            def pool_out(g, rows=0):
                cols = token_cols(g)
                for d in range(KD):
                    dot(rows)
                    bank = filled(dve, g, "pool_out", d)
                    nc.vector.tensor_tensor(merged[:, d, cols], gate_pool[:, d, cols],
                                            bank[:, 0:cols.stop - cols.start],
                                            ALU.mult).then_inc(frees(g, "pool_out", d), 1)

            def row_max(g, i):
                bank = filled(dve, g, "s", i)
                if i >= 2:
                    dve.wait_ge(exp_ready, STEPS_BEFORE[g] + i - 1)
                nc.vector.tensor_reduce(neg_max[:, i % 2:i % 2 + 1], bank[:], AX.X, ALU.max,
                                        negate=True).then_inc(max_ready, 1)

            def invert_sum(g, i):
                dve.wait_ge(exp_ready, STEPS_BEFORE[g] + i + 1)
                total = prob_sum[:, i % 2:i % 2 + 1]
                nc.vector.reciprocal(total, total).then_inc(frees(g, "s", i), 1)
                if g == 0:
                    moved(dve, g, "s", i)
                    nc.vector.tensor_scalar(probs[:, i % 2, :], probs[:, i % 2, :], total,
                                            None, ALU.mult).then_inc(probs_ready, 1)

            def attention(g, rows=0):
                row_max(g, 0)
                for i in range(len(attention_steps(g))):
                    if i + 1 < len(attention_steps(g)):
                        row_max(g, i + 1)
                    dot(rows)
                    invert_sum(g, i)

            def attn_out(g, rows=0):
                cols = token_cols(g)
                for d in range(KD):
                    dot(rows)
                    moved(dve, g, "gate_attn", d)
                    bank = filled(dve, g, "attn_out", d)
                    a = gate_attn[:, d % 2, cols]
                    nc.vector.tensor_tensor(a, a, bank[:, 0:cols.stop - cols.start],
                                            ALU.mult).then_inc(frees(g, "attn_out", d), 1)
                    moved(dve, g, "attn_out", d)
                    nc.vector.tensor_tensor(merged[:, d, cols], merged[:, d, cols], a,
                                            ALU.add).then_inc(merged_ready, 1)

            def out(g, rows=0):
                b = GROUP_OF[g][0]
                dve.wait_ge(res_loaded, 16 * (g + 1))
                for c in range(D // CHUNK):
                    for tp in tile_pairs(g):
                        dot(rows)
                        bank = filled(dve, g, "out", c, tp)
                        x = x1s[b][:, tp[0]:tp[-1] + 1, c * CHUNK:(c + 1) * CHUNK]
                        nc.vector.tensor_tensor(x, x, bank[:, 0:len(tp) * CHUNK].rearrange("p (t n) -> p t n", n=CHUNK),
                                                ALU.add).then_inc(frees(g, "out", c, tp), 1)
                for c in range(D // CHUNK):
                    for tp in tile_pairs(g):
                        moved(dve, g, "out", c, tp)
                dve.sem_inc(x1_ready, 1)

            def norm2(g):
                b, tiles = GROUP_OF[g]
                if g == 0:
                    dve.wait_ge(g_loaded, 16)
                dve.wait_ge(std2_ready, g + 1)
                st = stat[:, 1, tiles[0]:tiles[-1] + 1]
                link(nc.vector.reciprocal(st, st))
                for t in tiles:
                    nc.vector.scalar_tensor_tensor(out=h2_to_turn[b][:, t, :], in0=x1s[b][:, t, :],
                                                   scalar=stat[:, 1, t:t + 1], in1=g_row[:], op0=ALU.mult,
                                                   op1=ALU.mult).then_inc(h2_ready, 1)
                if b:
                    dve.wait_ge(h2_ready, TILES_BEFORE[g + 1])
                    for t in range(GATHERED[b]):
                        link(nc.vector.tensor_copy(h2[:, t, :], h2_to_turn[b][:, t, :]))

            def top_halves(g, hp):
                moved(dve, g, "keys", hp)
                s = score[:, hp % 4]
                tiles = GROUP_OF[g][1]
                ns = [step(nc.vector.max(best[:, t, hp, 0:8], s[:, n, :])) for n, t in enumerate(tiles)]
                for n, t in enumerate(tiles):
                    after(ns[n])
                    ns[n] = step(nc.vector.max_index(best_at[:, t, hp, 0:8], best[:, t, hp, 0:8], s[:, n, :]))
                for n, t in enumerate(tiles):
                    after(ns[n])
                    ns[n] = step(nc.vector.match_replace(s[:, n, :], best[:, t, hp, 0:8], s[:, n, :], LOWEST))
                for n, t in enumerate(tiles):
                    after(ns[n])
                    ns[n] = step(nc.vector.max(best[:, t, hp, 8:16], s[:, n, :]))
                for n, t in enumerate(tiles):
                    after(ns[n])
                    ins = nc.vector.max_index(best_at[:, t, hp, 8:16], best[:, t, hp, 8:16], s[:, n, :])
                ins.then_inc(halves_done, 1)

            def candidates(out, first, second):
                for a, rows, cols, off in CAND_RUNS:
                    dst = out[:, :, off:off + rows * cols]
                    left, right = first[:, :, a:a + rows], second[:, :, 0:cols]
                    if cols == 1:
                        right = right.to_broadcast([P, PEER_HEADS, rows])
                    elif rows == 1:
                        left = left.to_broadcast([P, PEER_HEADS, cols])
                    else:
                        dst = dst.rearrange("p h (a b) -> p h a b", b=cols)
                        left = left.unsqueeze(3).to_broadcast([P, PEER_HEADS, rows, cols])
                        right = right.unsqueeze(2).to_broadcast([P, PEER_HEADS, rows, cols])
                    step(nc.vector.tensor_tensor(dst, left, right, ALU.add))

            def merge(b, t, rows=0):
                g = next(n for n, (bb, tiles) in enumerate(GROUP_OF) if bb == b and t in tiles)
                if t == GROUP_OF[g][1][0]:
                    dve.wait_ge(halves_done, HALVES * (g + 1))
                ids = sel_f
                view = best_at[:, t].rearrange("p (h a) k -> p h a k", a=2)
                idv = ids.rearrange("p (h a) k -> p h a k", a=2)
                val = best[:, t].rearrange("p (h a) k -> p h a k", a=2)
                step(nc.vector.tensor_scalar(idv[:, :, 0, :], view[:, :, 0, :], float(N_KEYS), None, ALU.mult))
                step(nc.vector.tensor_copy(idv[:, :, 1, :], view[:, :, 1, :]))
                candidates(cand, val[:, :, 0, :], val[:, :, 1, :])
                sync()
                candidates(cand_id, idv[:, :, 0, :], idv[:, :, 1, :])
                top = gate[:, b, t, :].rearrange("p (h k) -> p h k", k=TOPK)
                pos_i = best_at[:, t].rearrange("p (a h) k -> p a h k", a=2)[:, 0]
                ns = [step(nc.vector.max(top[:, h, 0:8], cand[:, h, :])) for h in range(PEER_HEADS)]
                dot(rows // 2)
                for h in range(PEER_HEADS):
                    after(ns[h])
                    ns[h] = step(nc.vector.max_index(pos_i[:, h, 0:8], top[:, h, 0:8], cand[:, h, :]))
                dot(rows // 2)
                for h in range(PEER_HEADS):
                    after(ns[h])
                    ns[h] = step(nc.vector.match_replace(cand[:, h, :], top[:, h, 0:8], cand[:, h, :], LOWEST))
                dot(rows // 2)
                for h in range(PEER_HEADS):
                    after(ns[h])
                    ns[h] = step(nc.vector.max(top[:, h, 8:16], cand[:, h, :]))
                for h in range(PEER_HEADS):
                    after(ns[h])
                    step(nc.vector.max_index(pos_i[:, h, 8:16], top[:, h, 8:16], cand[:, h, :]))
                sync()
                pos = sel_f[:, 0:PEER_HEADS, :]
                found = sel_f[:, PEER_HEADS:, :]
                link(nc.vector.tensor_copy(pos, pos_i))
                hits = [m.rearrange("p (k n) -> p k n", n=CAND) for m in match]
                ns = [n_dve[0]] * 2
                for h0 in range(0, PEER_HEADS, 2):
                    dot(rows)
                    for n, (h, hit) in enumerate(zip((h0, h0 + 1), hits)):
                        after(ns[n])
                        ns[n] = step(nc.vector.tensor_tensor(
                            hit, pos[:, h, :].unsqueeze(2).to_broadcast([P, TOPK, CAND]),
                            iota[:, 0:CAND].unsqueeze(1).to_broadcast([P, TOPK, CAND]), ALU.is_equal))
                    for n, (h, hit) in enumerate(zip((h0, h0 + 1), hits)):
                        after(ns[n])
                        ns[n] = step(nc.vector.tensor_tensor(
                            hit, hit, cand_id[:, h:h + 1, :].to_broadcast([P, TOPK, CAND]), ALU.mult))
                    for n, (h, hit) in enumerate(zip((h0, h0 + 1), hits)):
                        after(ns[n])
                        ns[n] = step(nc.vector.tensor_reduce(found[:, h, :], hit, AX.X, ALU.add))
                sync()
                nc.vector.tensor_copy(idx[:, b, t * SLOTS:(t + 1) * SLOTS].rearrange("p (h k) -> p h k", k=TOPK),
                                      found).then_inc(idx_ready, 1)
                link(nc.vector.tensor_copy(cand[:, :, 0:1], top[:, :, 0:1]))
                nc.vector.tensor_tensor(top, top, cand[:, :, 0:1].to_broadcast([P, PEER_HEADS, TOPK]),
                                        ALU.subtract).then_inc(top_ready, 1)
                dve.wait_ge(top_ready, b * TT + t + 1)

            def softmax(b):
                dve.wait_ge(top_exp, b + 1)
                top = gate[:, b].rearrange("p t (h k) -> p (t h) k", k=TOPK)
                link(nc.vector.tensor_reduce(gate_sum[:], top, AX.X, ALU.add))
                link(nc.vector.reciprocal(gate_sum[:], gate_sum[:]))
                link(nc.vector.tensor_tensor(top, top, gate_sum[:].unsqueeze(2).to_broadcast(
                    [P, TT * PEER_HEADS, TOPK]), ALU.mult))

            def weigh_column(j, u, c):
                dve.wait_ge(col_moved, j + 1)
                w = weights_in[u].rearrange("p (b j t) -> p b j t", j=UNIT_COLS, t=BLOCK)
                h = hidden[c % 2].rearrange("p (b t) -> p b t", t=BLOCK)
                nc.vector.tensor_tensor(h, h, w[:, :, c, :], ALU.mult).then_inc(hidden_ready, 1)

            def rows_and_columns(b, phase, t, i, size, take_row, first=0):
                start = PHASE_START[b, phase] + t * SLOTS + first
                turn = (t - (SUMMED if (b, phase) == (0, 1) else 0)) * LONGS
                units = UNITS_BESIDE.get((b, phase), 0)
                cols = units * UNIT_COLS
                for s in range(size):
                    r = s % RING
                    dve.wait_ge(row_landed[r], (i * (size // RING) + (start // RING + s // RING + 1)) * 16)
                    take_row(i, s, r, start)
                    if (s + 1) * cols // size > s * cols // size:
                        n = s * cols // size
                        u, c = n // UNIT_COLS, n % UNIT_COLS
                        if c == 0:
                            dve.wait_ge(weights_loaded[u], (i + (PLACE_LOADS[b, phase][u] + turn + 1)) * 16)
                        weigh_column(i * cols + (UNITS_START[b, phase] * UNIT_COLS + turn * cols + n), u, c)

            def dot_rows(b, t, first, size, count):
                dots_before = b * GATHERED[0] * SLOTS // BODY + (t * SLOTS + first) // BODY

                def take(i, s, r, start):
                    nc.vector.tensor_tensor_reduce(ring[:, r, :], ring[:, r, :], h2[:, t, :], 1.0, 0.0, ALU.mult,
                                                   ALU.add, dots_now[:, s % BODY:s % BODY + 1]).then_inc(rows_used, 1)
                    if s % BODY == BODY - 1:
                        dve.wait_ge(rows_used, i * size + (RING + start + s + 1))
                        nc.vector.tensor_copy(dots[:, bass.ds(i * size + (t * SLOTS + first + s + 1 - BODY), BODY)],
                                              dots_now[:]).then_inc(dots_saved, 1)
                        dve.wait_ge(dots_saved, i * (size // BODY) + (dots_before + s // BODY + 1))

                with dve.Fori(0, count) as i:
                    rows_and_columns(b, 0, t, i, size, take, first)

            def weigh(b):
                dve.wait_ge(gelu_ready, b + 1)
                n = GATHERED[b]
                d = dots[:, 0:n * SLOTS]
                nc.vector.tensor_tensor(d, d, gate[:, b, 0:n].rearrange("p t n -> p (t n)"),
                                        ALU.mult).then_inc(weighed, 1)
                dve.wait_ge(weighed, b + 1)

            def add_rows(b, t):
                def take(i, s, r, start):
                    dve.wait_ge(rows_used, i * LONG + (RING + start + s))
                    nc.vector.scalar_tensor_tensor(
                        out=x1s[b][:, t, :], in0=ring[:, r, :],
                        scalar=dots[:, bass.ds(i * LONG + (t * SLOTS + s), 1)],
                        in1=x1s[b][:, t, :], op0=ALU.mult, op1=ALU.add).then_inc(rows_used, 1)

                with dve.Fori(0, LONGS) as i:
                    rows_and_columns(b, 1, t, i, LONG, take)

            def add_sums():
                dve.wait_ge(rows_used, RING + PHASE_START[0, 1] + SUMMED * SLOTS)
                for n in range(2):
                    x = x1s[0][:, 0, n * 512:(n + 1) * 512]
                    nc.vector.tensor_tensor(x, x, banks[JOB[LAST_GROUP[1], "sums", n] % BANKS][:],
                                            ALU.add).then_inc(frees(LAST_GROUP[1], "sums", n), 1)
                for n in range(2):
                    moved(dve, LAST_GROUP[1], "sums", n)
                dve.sem_inc(sums_added, 1)

            def split_ids(t):
                ids = idx[:, 1, t * SLOTS:(t + 1) * SLOTS]
                for a, (op, imm) in enumerate(((ALU.logical_shift_right, 7), (ALU.bitwise_and, N_KEYS - 1))):
                    link(nc.vector.tensor_scalar(part_u, ids, imm, None, op))
                    link(nc.vector.tensor_copy(parts[:, t - GATHERED[1], a, :], part_u))
                dve.sem_inc(parts_ready, 1)

            def one_hots(block):
                if block == 0:
                    for t in range(GATHERED[1], TT):
                        moved(dve, LAST_GROUP[1], "chosen", t)
                with dve.Fori(0, BLOCK // OH_RING) as i:
                    for r in range(OH_RING):
                        n = i * OH_RING + (block * BLOCK + r)
                        col = bass.ds(n, 1)
                        if r % 4 == 0:
                            dve.wait_ge(block_filled[r // 4], i + (block * BLOCK // OH_RING + 1))
                            nc.vector.tensor_tensor(one_hot_i[:, r:r + 4, :],
                                                    iota[:].unsqueeze(1).to_broadcast([P, 4, N_KEYS]),
                                                    chosen[:, 0, bass.ds(n, 4)].unsqueeze(2).to_broadcast(
                                                        [P, 4, N_KEYS]), ALU.is_equal)
                        nc.vector.tensor_scalar(one_hot_j[:, r, :], iota[:], chosen[:, 1, col], chosen[:, 2, col],
                                                ALU.is_equal, ALU.mult).then_inc(one_hot_ready, 1)

            def add_dense():
                dve.wait_ge(col_added, N_KEYS + 2)
                for t in range(GATHERED[1], TT):
                    for n in range(2):
                        x = x1s[1][:, t, n * 512:(n + 1) * 512]
                        step(nc.vector.tensor_tensor(x, x, dense_out[2 * (t - GATHERED[1]) + n][:], ALU.add))
                    sync()
                    dve.sem_inc(dense_added, 1)

            def finish(b, t):
                dve.wait_ge(g_loaded, 32)
                dve.wait_ge(std3_ready, b * TT + t + 1)
                link(nc.vector.reciprocal(stat[:, 2, t:t + 1], stat[:, 2, t:t + 1]))
                nc.vector.scalar_tensor_tensor(out=x1s[b][:, t, :], in0=x1s[b][:, t, :], scalar=stat[:, 2, t:t + 1],
                                               in1=g_row[:], op0=ALU.mult, op1=ALU.mult).then_inc(y_ready, 1)

            step(nc.vector.memset(eps[:], EPS))
            dve.sem_inc(rows_used, RING)
            norm1(0)
            rotate(0)
            pool_out(0)
            attention(0)
            attn_out(0)
            out(0)
            norm2(0)
            for hp in range(HALVES):
                top_halves(0, hp)
            merge(0, 0)

            pool_out(1)
            attention(1, 1)
            attn_out(1, 3)
            out(1, 3)
            dot(4)
            norm2(1)
            dot(4)
            for hp in range(HALVES):
                top_halves(1, hp)
                dot(2)
            norm1(1)
            merge(0, 1, 3)
            dot_to(8)
            merge(0, 2, 6)
            merge(0, 3, 6)
            rotate(1, 3)
            pool_out(2, 3)
            attention(2, 3)
            attn_out(2, 7)
            out(2, 5)
            dot(4)
            norm2(2)
            dot(8)
            for hp in range(HALVES):
                top_halves(2, hp)
                dot(4)
            dot_to(GATHERED[0] * SLOTS // BODY)
            softmax(0)
            weigh(0)
            for t in range(TT):
                merge(1, t)
            softmax(1)
            for t in range(GATHERED[1], TT):
                split_ids(t)
            for block in range(BLOCKS):
                one_hots(block)
            add_sums()
            for t in range(SUMMED, TT):
                add_rows(0, t)
            for t in range(TT):
                finish(0, t)
            for t in range(GATHERED[1]):
                dot_rows(1, t, 0, LONG, LONGS)
            weigh(1)
            for t in range(GATHERED[1]):
                add_rows(1, t)
                finish(1, t)
            add_dense()
            for t in range(GATHERED[1], TT):
                finish(1, t)


def shape_constants(np):
    band = np.zeros((P, GROUPS, BAND_W), np.float32)
    s, t = np.arange(T)[:, None], np.arange(T)[None, :]
    for g, w in enumerate(WINDOWS):
        lo, hi = np.clip(t - w // 2, 0, T), np.clip(t + w - w // 2, 0, T)
        m = ((s >= lo) & (s < hi)) / (hi - lo).astype(np.float32) - (s == t)
        for kind, tile in enumerate((0, 1, TT - 1)):
            band[:, g, kind * P:(kind + 1) * P] = m[tile * P:(tile + 1) * P, tile * P:(tile + 1) * P]
        band[:, g, 3 * P:3 * P + EDGE] = m[0:P, P:P + EDGE]
        band[:, g, 3 * P + EDGE:] = m[P:2 * P, P - EDGE:P]
    quarter = HD // 4
    inv = np.float32(ROPE_THETA) ** (-np.arange(quarter, dtype=np.float32) / np.float32(quarter))
    rope = np.zeros((P, TT, 2, 2, 2, quarter), np.float32)
    tok = np.arange(T).reshape(TT, P).T
    for axis, pos in enumerate((tok // GRID_W, tok % GRID_W)):
        ang = pos.astype(np.float32)[:, :, None] * inv.astype(np.float32)
        rope[:, :, 0, axis] = np.cos(ang)[:, :, None]
        rope[:, :, 1, axis, 0] = -np.sin(ang)
        rope[:, :, 1, axis, 1] = np.sin(ang)
    iota = np.broadcast_to(np.arange(P, dtype=np.float32), (P, P))
    return {"ident_c": np.eye(P, dtype=np.float32), "band_c": band,
            "rope_c": rope.reshape(P, TT, 2, HD), "iota_c": np.ascontiguousarray(iota)}


def kernel(**inputs):
    import numpy as np
    import concourse.bacc as bacc
    from concourse.bass_utils import run_bass_kernel_spmd

    a = {k: np.asarray(v) for k, v in inputs.items()}
    columns = lambda v, n: np.ascontiguousarray(v.reshape(n, P).T)
    arrays = {
        "x_prompt": a["x_prompt"], "x_sample": a["x_sample"], "w_in": a["w_in"][0], "pool_w": a["pool_w"][0],
        "w_pool_out": a["w_pool_out"][0], "w_attn_out": a["w_attn_out"][0], "w_out": a["w_out"][0],
        "w_query": a["w_query"][0],
        "keysT": a["sub_keys"][0].reshape(HALVES * N_KEYS, P).T,
        "expert_u": a["expert_u"][0], "expert_v": a["expert_v"][0],
        "expert_uT": a["expert_u"][0].reshape(N_KEYS, N_KEYS, KD, P).transpose(3, 1, 2, 0).reshape(P, N_KEYS, D),
        "g_mix": columns(a["g_mix"][0], KD), "pool_scale": columns(a["pool_scale"][0], GROUPS),
        "q_norm": a["q_norm"][0], "k_norm": a["k_norm"][0], "g_ffn": a["g_ffn"][0], "g_final": a["g_final"],
        **shape_constants(np),
    }
    nc = bacc.Bacc("TRN2", target_bir_lowering=False, num_devices=1)
    given, args = {}, []
    for name, v in arrays.items():
        v = np.ascontiguousarray(v)
        given[f"in_{name}"] = v
        args.append(nc.dram_tensor(f"in_{name}", v.shape, mybir.dt.from_np(v.dtype), kind="ExternalInput").ap())
    for n in range(BATCHES):
        args.append(nc.dram_tensor(f"out_{n}", (1, T, D), F32, kind="ExternalOutput").ap())
    encoder_kernel(nc, *args)
    r = run_bass_kernel_spmd(nc, [given], core_ids=[0])
    return tuple(r.results[0][f"out_{n}"] for n in range(BATCHES))
```
